# Optimizing a Trainium2 kernel written in Bass

```python
import math
import jax
import jax.numpy as jnp
from jax import lax
import numpy as np

D_MODEL = 1024
BATCH = 1
SEQ = 256
DEPTH = 4

GRID_W = 64
CTX_LEN = 256
N_MIXERS = 3
Q_BLOCK = 128
ROPE_THETA = 10000.0
EPS = 1e-6
NEG_INF = -1e30
CONV_WIDTH = 3
N_MOD = 6

A_HEADS = 8
A_KV_HEADS = 2
A_HEAD_DIM = D_MODEL // A_HEADS

FILTER_BANDS = 16
FILTER_EMB_DIM = 1 + 2 * FILTER_BANDS
FILTER_WIDTH = 64
FILTER_SIN_FREQ = 1.0
DECAY_TARGET = 1e-2
DECAY_FAST_PCT = 0.3
DECAY_SLOW_PCT = 1.5

C_HEADS = 16
C_KV_HEADS = 2
C_HEAD_DIM = D_MODEL // C_HEADS
WINDOW = 128

D_FF = 2816

N_A = (DEPTH + 2) // 3
N_B = (DEPTH + 1) // 3
N_C = DEPTH // 3

kernel_name = "hybrid_interleaved_dit_ctx_prefix"

def _rmsnorm(x, g):
    xf = x.astype(jnp.float32)
    y = xf * lax.rsqrt(jnp.mean(xf * xf, axis=-1, keepdims=True) + EPS)
    return (y * g.astype(jnp.float32)).astype(x.dtype)

def _modulate(x, shift, scale):
    return x * (1.0 + scale) + shift

def _dwconv(u, w, b):
    half = CONV_WIDTH // 2
    l = u.shape[1]
    up = jnp.pad(u, ((0, 0), (half, half), (0, 0)))
    out = b
    for j in range(CONV_WIDTH):
        out = out + up[:, j:j + l] * w[j]
    return out

def _axial_rope(seq_len, head_dim):
    rows = seq_len // GRID_W
    row = jnp.repeat(jnp.arange(rows), GRID_W).astype(jnp.float32)
    col = jnp.tile(jnp.arange(GRID_W), rows).astype(jnp.float32)
    axis_dim = head_dim // 2
    inv = jnp.power(ROPE_THETA, -jnp.arange(0, axis_dim, 2, dtype=jnp.float32) / axis_dim)
    ang = jnp.concatenate([row[:, None] * inv[None], col[:, None] * inv[None]], axis=-1)
    return jnp.cos(ang), jnp.sin(ang)

def _rope(x, cos, sin):
    half = x.shape[-1] // 2
    shape = (cos.shape[0],) + (1,) * (x.ndim - 3) + (half,)
    cos = cos.reshape(shape).astype(x.dtype)
    sin = sin.reshape(shape).astype(x.dtype)
    x1, x2 = x[..., :half], x[..., half:]
    return jnp.concatenate([x1 * cos - x2 * sin, x1 * sin + x2 * cos], axis=-1)

def _project(h, w, bias, n_heads, n_kv, head_dim, with_q):
    q_cols = n_heads * head_dim
    if not with_q:
        w = w[:, q_cols:]
        bias = None if bias is None else bias[q_cols:]
    out = h @ w
    if bias is not None:
        out = out + bias
    bsz, l, _ = h.shape
    q = None
    if with_q:
        q = out[..., :q_cols].reshape(bsz, l, n_kv, n_heads // n_kv, head_dim)
        out = out[..., q_cols:]
    k, v = jnp.split(out, 2, axis=-1)
    return q, k.reshape(bsz, l, n_kv, head_dim), v.reshape(bsz, l, n_kv, head_dim)

def _dense_block_attention(q, k, v, scale):
    b, l, nkv, g, dh = q.shape
    nb = l // Q_BLOCK
    qb = jnp.moveaxis(q.reshape(b, nb, Q_BLOCK, nkv, g, dh), 1, 0)

    def one_block(qi):
        s = jnp.einsum('bqkgd,bskd->bkgqs', qi, k).astype(jnp.float32) * scale
        p = jax.nn.softmax(s, axis=-1).astype(v.dtype)
        return jnp.einsum('bkgqs,bskd->bqkgd', p, v)

    ob = lax.map(one_block, qb)
    return jnp.moveaxis(ob, 0, 1).reshape(b, l, nkv, g, dh)

def _sink_attention(q, k, v, sink_logit, scale):
    s = jnp.einsum('bqkgd,bskd->bkgqs', q, k).astype(jnp.float32) * scale
    s0 = jnp.broadcast_to(sink_logit[None, :, :, None, None], s.shape[:-1] + (1,))
    p = jax.nn.softmax(jnp.concatenate([s0, s], axis=-1), axis=-1)[..., 1:].astype(v.dtype)
    return jnp.einsum('bkgqs,bskd->bqkgd', p, v)

def _window_attention(q, k, v, kc, vc, sink_logit, scale):
    b, l, nkv, g, dh = q.shape
    nb = l // Q_BLOCK
    n_ctx = kc.shape[1]

    def band(t):
        tp = jnp.pad(t, ((0, 0), (Q_BLOCK, Q_BLOCK), (0, 0), (0, 0))).reshape(b, nb + 2, Q_BLOCK, nkv, dh)
        return jnp.concatenate([tp[:, :-2], tp[:, 1:-1], tp[:, 2:]], axis=2)

    kb, vb = band(k), band(v)
    qb = q.reshape(b, nb, Q_BLOCK, nkv, g, dh)
    offs = jnp.arange(3 * Q_BLOCK)[None, :] - Q_BLOCK
    rel = offs - jnp.arange(Q_BLOCK)[:, None]
    key_pos = jnp.arange(nb)[:, None] * Q_BLOCK + offs
    valid = (jnp.abs(rel) <= WINDOW)[None] & ((key_pos >= 0) & (key_pos < l))[:, None, :]

    def one_block(args):
        qi, ki, vi, mi = args
        s_loc = jnp.einsum('bqkgd,bskd->bkgqs', qi, ki).astype(jnp.float32) * scale
        s_loc = jnp.where(mi, s_loc, NEG_INF)
        s_ctx = jnp.einsum('bqkgd,bskd->bkgqs', qi, kc).astype(jnp.float32) * scale
        s0 = jnp.broadcast_to(sink_logit[None, :, :, None, None], s_ctx.shape[:-1] + (1,))
        p = jax.nn.softmax(jnp.concatenate([s0, s_ctx, s_loc], axis=-1), axis=-1).astype(v.dtype)
        return (jnp.einsum('bkgqs,bskd->bqkgd', p[..., 1:1 + n_ctx], vc)
                + jnp.einsum('bkgqs,bskd->bqkgd', p[..., 1 + n_ctx:], vi))

    ob = lax.map(one_block, (jnp.moveaxis(qb, 1, 0), jnp.moveaxis(kb, 1, 0), jnp.moveaxis(vb, 1, 0), valid))
    return jnp.moveaxis(ob, 0, 1).reshape(b, l, nkv, g, dh)

def _mixer_a(h_lat, h_ctx, w_qkv, q_gain, k_gain, w_out, cos, sin, need_ctx):
    scale = A_HEAD_DIM ** -0.5
    b, l, _ = h_lat.shape
    q, k, v = _project(h_lat, w_qkv, None, A_HEADS, A_KV_HEADS, A_HEAD_DIM, True)
    q = _rope(_rmsnorm(q, q_gain), cos, sin)
    k = _rope(_rmsnorm(k, k_gain), cos, sin)
    qc, kc, vc = _project(h_ctx, w_qkv, None, A_HEADS, A_KV_HEADS, A_HEAD_DIM, need_ctx)
    kc = _rmsnorm(kc, k_gain)
    k_all = jnp.concatenate([kc, k], axis=1)
    v_all = jnp.concatenate([vc, v], axis=1)
    o_lat = _dense_block_attention(q, k_all, v_all, scale).reshape(b, l, A_HEADS * A_HEAD_DIM) @ w_out
    o_ctx = None
    if need_ctx:
        oc = _dense_block_attention(_rmsnorm(qc, q_gain), kc, vc, scale)
        o_ctx = oc.reshape(b, h_ctx.shape[1], A_HEADS * A_HEAD_DIM) @ w_out
    return o_lat, o_ctx

def _hyena_filter(seq_len, w1, b1, w2, b2, w3, b3, w4):
    t = jnp.linspace(0.0, 1.0, seq_len, dtype=jnp.float32)[:, None]
    omega = (2.0 * math.pi / seq_len) * jnp.arange(seq_len, dtype=jnp.float32)
    bands = jnp.linspace(1e-4, FILTER_BANDS - 1, FILTER_BANDS, dtype=jnp.float32)
    ang = omega[:, None] * bands[None, :]
    z = jnp.concatenate([t, jnp.cos(ang), -jnp.sin(ang)], axis=-1)
    f = jnp.sin(FILTER_SIN_FREQ * (z @ w1 + b1))
    f = jnp.sin(FILTER_SIN_FREQ * (f @ w2 + b2))
    f = jnp.sin(FILTER_SIN_FREQ * (f @ w3 + b3))
    f = (f @ w4).astype(jnp.float32)
    rates = jnp.abs(jnp.linspace(math.log(DECAY_TARGET) / DECAY_FAST_PCT,
                                 math.log(DECAY_TARGET) / DECAY_SLOW_PCT, D_MODEL, dtype=jnp.float32))
    decay = jnp.exp(-t * rates[None, :])
    return f[:, :D_MODEL] * decay, f[:, D_MODEL:] * decay

def _bidir_long_conv(u, h_fwd, h_bwd, skip):
    l = u.shape[1]
    n = 2 * l
    filt = jnp.concatenate([h_fwd, jnp.zeros_like(h_fwd[:1]), h_bwd[:0:-1]], axis=0)
    uf = jnp.fft.rfft(u.astype(jnp.float32), n=n, axis=1)
    ff = jnp.fft.rfft(filt, n=n, axis=0)
    y = jnp.fft.irfft(uf * ff[None], n=n, axis=1)[:, :l]
    return (y + u.astype(jnp.float32) * skip.astype(jnp.float32)).astype(u.dtype)

def _hyena_mixer(h, w_in, b_in, conv_w, conv_b, f_w1, f_b1, f_w2, f_b2, f_w3, f_b3, f_w4, skip, w_out, b_out):
    u = _dwconv(h @ w_in + b_in, conv_w, conv_b)
    x0, x1, v = jnp.split(u, 3, axis=-1)
    h_fwd, h_bwd = _hyena_filter(h.shape[1], f_w1, f_b1, f_w2, f_b2, f_w3, f_b3, f_w4)
    v = _bidir_long_conv(v * x1, h_fwd, h_bwd, skip)
    return (v * x0) @ w_out + b_out

def _mixer_c(h_lat, h_ctx, w_qkv, b_qkv, sink, w_out, b_out, cos, sin, need_ctx):
    scale = C_HEAD_DIM ** -0.5
    b, l, _ = h_lat.shape
    q, k, v = _project(h_lat, w_qkv, b_qkv, C_HEADS, C_KV_HEADS, C_HEAD_DIM, True)
    q, k = _rope(q, cos, sin), _rope(k, cos, sin)
    qc, kc, vc = _project(h_ctx, w_qkv, b_qkv, C_HEADS, C_KV_HEADS, C_HEAD_DIM, need_ctx)
    sink_logit = sink.reshape(C_KV_HEADS, C_HEADS // C_KV_HEADS).astype(jnp.float32)
    o = _window_attention(q, k, v, kc, vc, sink_logit, scale)
    o_lat = o.reshape(b, l, C_HEADS * C_HEAD_DIM) @ w_out + b_out
    o_ctx = None
    if need_ctx:
        oc = _sink_attention(qc, kc, vc, sink_logit, scale)
        o_ctx = oc.reshape(b, h_ctx.shape[1], C_HEADS * C_HEAD_DIM) @ w_out + b_out
    return o_lat, o_ctx

def _conv_ffn(h, w_up, conv_w, conv_b, w_down):
    gate, up = jnp.split(h @ w_up, 2, axis=-1)
    return (jax.nn.silu(_dwconv(gate, conv_w, conv_b)) * up) @ w_down

def setup_inputs(seed: int = 0) -> dict:
    key = jax.random.key(seed)
    ks = iter(jax.random.split(key, 40))

    def nrm(shape, scale=1.0):
        return jax.random.normal(next(ks), shape, jnp.float32) * scale

    d = D_MODEL
    a_cols = (A_HEADS + 2 * A_KV_HEADS) * A_HEAD_DIM
    c_cols = (C_HEADS + 2 * C_KV_HEADS) * C_HEAD_DIM
    return {
        'x': nrm((BATCH, SEQ, d)),
        'c': nrm((BATCH, d)),
        'ctx': nrm((BATCH, CTX_LEN, d)),
        'c_ctx': nrm((d,)),
        'mod_w': nrm((DEPTH, d, N_MOD * d), d ** -0.5),
        'mod_b': nrm((DEPTH, N_MOD * d), 0.02),
        'norm_g': 1.0 + nrm((DEPTH, 4, d), 0.05),
        'ffn_w_up': nrm((DEPTH, d, 2 * D_FF), d ** -0.5),
        'ffn_conv_w': nrm((DEPTH, CONV_WIDTH, D_FF), CONV_WIDTH ** -0.5),
        'ffn_conv_b': nrm((DEPTH, D_FF), 0.02),
        'ffn_w_down': nrm((DEPTH, D_FF, d), D_FF ** -0.5),
        'a_w_qkv': nrm((N_A, d, a_cols), d ** -0.5),
        'a_q_gain': 1.0 + nrm((N_A, A_HEAD_DIM), 0.05),
        'a_k_gain': 1.0 + nrm((N_A, A_HEAD_DIM), 0.05),
        'a_w_out': nrm((N_A, A_HEADS * A_HEAD_DIM, d), (A_HEADS * A_HEAD_DIM) ** -0.5),
        'b_w_in': nrm((N_B, d, 3 * d), d ** -0.5),
        'b_b_in': nrm((N_B, 3 * d), 0.02),
        'b_conv_w': nrm((N_B, CONV_WIDTH, 3 * d), CONV_WIDTH ** -0.5),
        'b_conv_b': nrm((N_B, 3 * d), 0.02),
        'b_f_w1': nrm((N_B, FILTER_EMB_DIM, FILTER_WIDTH), FILTER_EMB_DIM ** -0.5),
        'b_f_b1': nrm((N_B, FILTER_WIDTH), 0.1),
        'b_f_w2': nrm((N_B, FILTER_WIDTH, FILTER_WIDTH), FILTER_WIDTH ** -0.5),
        'b_f_b2': nrm((N_B, FILTER_WIDTH), 0.1),
        'b_f_w3': nrm((N_B, FILTER_WIDTH, FILTER_WIDTH), FILTER_WIDTH ** -0.5),
        'b_f_b3': nrm((N_B, FILTER_WIDTH), 0.1),
        'b_f_w4': nrm((N_B, FILTER_WIDTH, 2 * d), FILTER_WIDTH ** -0.5),
        'b_skip': nrm((N_B, d)),
        'b_w_out': nrm((N_B, d, d), d ** -0.5),
        'b_b_out': nrm((N_B, d), 0.02),
        'c_w_qkv': nrm((N_C, d, c_cols), d ** -0.5),
        'c_b_qkv': nrm((N_C, c_cols), 0.02),
        'c_sink': nrm((N_C, C_HEADS)),
        'c_w_out': nrm((N_C, C_HEADS * C_HEAD_DIM, d), (C_HEADS * C_HEAD_DIM) ** -0.5),
        'c_b_out': nrm((N_C, d), 0.02),
    }

def reference(x, c, ctx, c_ctx, mod_w, mod_b, norm_g, ffn_w_up, ffn_conv_w, ffn_conv_b, ffn_w_down,
              a_w_qkv, a_q_gain, a_k_gain, a_w_out,
              b_w_in, b_b_in, b_conv_w, b_conv_b, b_f_w1, b_f_b1, b_f_w2, b_f_b2, b_f_w3, b_f_b3, b_f_w4,
              b_skip, b_w_out, b_b_out,
              c_w_qkv, c_b_qkv, c_sink, c_w_out, c_b_out):
    seq_len = x.shape[1]
    cos_a, sin_a = _axial_rope(seq_len, A_HEAD_DIM)
    cos_c, sin_c = _axial_rope(seq_len, C_HEAD_DIM)
    s_lat = jax.nn.silu(c)
    s_ctx = jax.nn.silu(c_ctx)
    h_lat, h_ctx = x, ctx
    for i in range(DEPTH):
        need_ctx = i < DEPTH - 1
        kind, j = i % N_MIXERS, i // N_MIXERS
        g = norm_g[i]
        m_lat = jnp.split((s_lat @ mod_w[i] + mod_b[i])[:, None, :], N_MOD, axis=-1)
        m_ctx = jnp.split(s_ctx @ mod_w[i] + mod_b[i], N_MOD, axis=-1)
        u_lat = _modulate(_rmsnorm(h_lat, g[0]), m_lat[0], m_lat[1])
        if kind == 0:
            u_ctx = _modulate(_rmsnorm(h_ctx, g[0]), m_ctx[0], m_ctx[1])
            o_lat, o_ctx = _mixer_a(u_lat, u_ctx, a_w_qkv[j], a_q_gain[j], a_k_gain[j], a_w_out[j],
                                    cos_a, sin_a, need_ctx)
        elif kind == 1:
            hy = (b_w_in[j], b_b_in[j], b_conv_w[j], b_conv_b[j], b_f_w1[j], b_f_b1[j], b_f_w2[j], b_f_b2[j],
                  b_f_w3[j], b_f_b3[j], b_f_w4[j], b_skip[j], b_w_out[j], b_b_out[j])
            o_lat = _hyena_mixer(u_lat, *hy)
            o_ctx = None
            if need_ctx:
                u_ctx = _modulate(_rmsnorm(h_ctx, g[0]), m_ctx[0], m_ctx[1])
                o_ctx = _hyena_mixer(u_ctx, *hy)
        else:
            u_ctx = _modulate(_rmsnorm(h_ctx, g[0]), m_ctx[0], m_ctx[1])
            o_lat, o_ctx = _mixer_c(u_lat, u_ctx, c_w_qkv[j], c_b_qkv[j], c_sink[j], c_w_out[j], c_b_out[j],
                                    cos_c, sin_c, need_ctx)
        ffn = (ffn_w_up[i], ffn_conv_w[i], ffn_conv_b[i], ffn_w_down[i])
        h_lat = h_lat + m_lat[2] * _rmsnorm(o_lat, g[1])
        f_lat = _conv_ffn(_modulate(_rmsnorm(h_lat, g[2]), m_lat[3], m_lat[4]), *ffn)
        h_lat = h_lat + m_lat[5] * _rmsnorm(f_lat, g[3])
        if need_ctx:
            h_ctx = h_ctx + m_ctx[2] * _rmsnorm(o_ctx, g[1])
            f_ctx = _conv_ffn(_modulate(_rmsnorm(h_ctx, g[2]), m_ctx[3], m_ctx[4]), *ffn)
            h_ctx = h_ctx + m_ctx[5] * _rmsnorm(f_ctx, g[3])
    return h_lat


_drawn_inputs = setup_inputs


def setup_inputs(seed=0):
    import zlib

    import numpy as np

    out = dict(_drawn_inputs(seed))
    spreads = {}
    factors = {'ffn_conv_b': 4.547,
     'a_q_gain': 4.871,
     'a_k_gain': 4.345,
     'b_b_in': 3.776,
     'b_conv_b': 4.085,
     'b_b_out': 23.629,
     'c_b_qkv': 4.864,
     'c_sink': 8.0,
     'c_b_out': 4.963}
    for name, (base, spread) in spreads.items():
        noise = np.random.default_rng([zlib.crc32(name.encode()), seed]).standard_normal(out[name].shape)
        drawn = base * np.exp(spread * noise) if base else spread * noise
        out[name] = jnp.asarray(drawn.astype(out[name].dtype))
    for name, factor in factors.items():
        out[name] = (out[name] * factor).astype(out[name].dtype)
    return out
```

```python
import math
from contextlib import ExitStack

import numpy as np

import concourse.bass as bass
from concourse import mybir

F32 = mybir.dt.float32
F32R = mybir.dt.float32r
ALU = mybir.AluOpType
ACT = mybir.ActivationFunctionType
AX = mybir.AxisListType

P = 128
D = 1024
KT = D // P
SEQ = 256
CTX = 256
TOK = SEQ + CTX
DEPTH = 4
GRID_W = 64
DFF = 2816
FM = DFF // P
EPS = 1e-6
TW = 256
A_HEADS, A_KV, A_DH = 8, 2, 128
C_HEADS, C_KV, C_DH = 16, 2, 64
FEMB, FW = 33, 64
NMOD = 6
MB = NMOD * D // TW
NFREQ = 2 * SEQ
KIND = [i % 3 for i in range(DEPTH)]

ROWS = [("norm_g", DEPTH * 4 * KT), ("ffn_conv_w", DEPTH * 3 * FM), ("ffn_conv_b", DEPTH * FM),
        ("mod_b", DEPTH * NMOD * KT), ("c", KT), ("c_ctx", KT), ("a_q_gain", 2), ("a_k_gain", 2),
        ("b_b_in", 3 * KT), ("b_conv_w", 9 * KT), ("b_conv_b", 3 * KT), ("b_skip", KT), ("b_b_out", KT),
        ("c_b_qkv", 10), ("c_b_out", KT)]
ROW0 = {}
_n = 0
for _name, _k in ROWS:
    ROW0[_name] = _n
    _n += _k
NPAR = -(-_n // P)

TILES = []
FIRST = {}
for _i in range(DEPTH):
    _k, _j = KIND[_i], _i // 3
    FIRST["in", _i] = len(TILES)
    if _k == 0:
        TILES += [("a_w_qkv", _j, 0, KT, TW * t, TW) for t in range(6)]
    elif _k == 1:
        TILES += [("b_w_in", _j, 0, KT, TW * t, TW) for t in range(4)]
        for _t in range(4):
            TILES += [("b_w_in", _j, 0, KT, D + TW * _t, TW), ("b_w_in", _j, 0, KT, 2 * D + TW * _t, TW)]
    else:
        TILES += [("c_w_qkv", _j, 0, KT, TW * t, TW) for t in range(4)]
        TILES += [("c_w_qkv", _j, 0, KT, D, P), ("c_w_qkv", _j, 0, KT, D + P, P)]
    FIRST["out", _i] = len(TILES)
    TILES += [("abc"[_k] + "_w_out", _j, 0, KT, TW * t, TW) for t in range(4)]
    FIRST["up", _i] = len(TILES)
    for _t in range(FM // 2):
        TILES += [("ffn_w_up", _i, 0, KT, TW * _t, TW), ("ffn_w_up", _i, 0, KT, DFF + TW * _t, TW)]
    FIRST["down", _i] = len(TILES)
    for _t in range(4):
        TILES += [("ffn_w_down", _i, r, min(8, FM - r), TW * _t, TW) for r in range(0, FM, 8)]
NT = len(TILES)


def constants():
    f = np.float32
    out = {}

    def rope(dh):
        axis = dh // 2
        inv = np.power(f(10000.0), -np.arange(0, axis, 2, dtype=f) / f(axis)).astype(f)
        t = np.arange(SEQ)
        ang = np.concatenate([(t // GRID_W).astype(f)[:, None] * inv[None],
                              (t % GRID_W).astype(f)[:, None] * inv[None]], axis=-1)
        half = dh // 2
        cos, sin = np.ones((P, TOK), f), np.zeros((P, TOK), f)
        for p in range(P):
            cos[p, :SEQ] = np.cos(ang[:, p % half]).astype(f)
            sin[p, :SEQ] = np.sin(ang[:, p % half]).astype(f)
        rot = np.zeros((P, P), f)
        for p in range(P):
            if p % dh < half:
                rot[p + half, p] = -1.0
            else:
                rot[p - half, p] = 1.0
        return cos, sin, rot

    cos, sin, rot = rope(A_DH)
    out["k_rope_a"] = np.concatenate([cos, sin, rot], axis=1)
    cos, sin, rot = rope(C_DH)
    mats = [rot]
    for kv in range(C_KV):
        dup = np.zeros((P, P), f)
        for p in range(P):
            dup[C_DH * kv + p % C_DH, p] = 1.0
        mats += [dup, (rot.astype(np.float64) @ dup).astype(f)]
    mask = np.zeros((2, P, TOK), f)
    for b in range(2):
        q = b * P + np.arange(P)[:, None]
        mask[b, :, :SEQ] = np.where(np.abs(np.arange(SEQ)[None, :] - q) <= 128, 0.0, -1e30)
    out["k_rope_c"] = np.concatenate([cos, sin] + mats + [mask[0], mask[1]], axis=1)
    out["k_ident"] = np.concatenate([np.eye(P, dtype=f), 1.0 - np.eye(P, 1, dtype=f)], axis=1)

    t = np.linspace(0.0, 1.0, SEQ, dtype=f)[:, None]
    omega = (f(2.0 * math.pi / SEQ) * np.arange(SEQ, dtype=f)).astype(f)
    bands = np.linspace(1e-4, 15, 16, dtype=f)
    ang = (omega[:, None] * bands[None, :]).astype(f)
    z = np.concatenate([t, np.cos(ang), -np.sin(ang)], axis=-1).astype(f)
    out["k_zt"] = np.ascontiguousarray(z.T)
    rates = np.abs(np.linspace(math.log(1e-2) / 0.3, math.log(1e-2) / 1.5, D, dtype=f))
    out["k_decay"] = np.exp(-t * rates[None, :]).astype(f)

    s = np.arange(SEQ, dtype=np.float64)[:, None]
    fr = np.arange(SEQ, dtype=np.float64)[None, :]
    th = 2 * np.pi * ((s * fr) % NFREQ) / NFREQ
    re, im = np.cos(th), -np.sin(th)
    nyq = np.cos(np.pi * s)
    imn = np.concatenate([nyq, im[:, 1:]], axis=1)
    ren = np.concatenate([nyq, re[:, 1:P]], axis=1)
    out["k_dft"] = np.concatenate([re, imn, ren, im[:, :P]], axis=1).astype(f)
    w = np.full((SEQ, 1), 2.0 / NFREQ)
    w[0] = 1.0 / NFREQ
    inv_re = w * np.cos(th.T)
    inv_im = -2.0 / NFREQ * np.sin(th.T)
    inv_im[0] = 1.0 / NFREQ * np.cos(np.pi * np.arange(SEQ))
    out["k_idft"] = np.concatenate([inv_re, inv_im], axis=0).astype(f)
    return out


def build(nc, a, out):
    es = ExitStack()
    with es:
        def sem(name):
            return es.enter_context(nc.semaphore(name))

        slab_words = 54400
        es.enter_context(nc.sbuf_tensor("slab", [P, slab_words + 8], F32))
        base = SLAB_AT
        cur = [base]

        def place(name, shape, dt=F32, at=None):
            n = -(-4 * math.prod(shape[1:]) // 32) * 32
            off = cur[0] if at is None else at
            if at is None:
                cur[0] += n
                assert cur[0] <= base + 4 * slab_words, (name, cur[0] - base, 4 * slab_words)
            return nc.alloc_sbuf_tensor_at(name, shape, dt, offset=off)

        H = place("h", [P, KT, TOK])
        U_AT = cur[0]
        UH = place("u_hi", [P, KT, TOK], F32R)
        UL = place("u_lo", [P, KT, TOK], F32R)
        M0 = cur[0]
        MH = place("mid_hi", [P, FM, TOK], F32R)
        ML = place("mid_lo", [P, FM, TOK], F32R)
        M_END = cur[0]
        RAW = place("w_raw", [P, 2, KT * TW])
        WH = place("w_hi", [P, 2, KT * TW], F32R)
        WL = place("w_lo", [P, 2, KT * TW], F32R)
        SQ_AT = cur[0]
        SQ = place("squares", [P, 2, TOK])
        CV = place("conv", [P, 2, TOK])
        MR = place("mod_raw", [P, 2, 4, TW])
        MA_AT = cur[0]
        MA = place("mod_acc", [P, 2, 2, TW])
        par = place("par", [P, NPAR * P])
        ident_t = place("ident", [P, P + 1])
        ones = place("ones", [P, P])
        S2 = place("silu_c", [P, 2, KT])
        modv = place("modv", [P, 2, NMOD * KT])
        coef = place("coef", [P, 2, 4, KT])
        small = place("small", [P, 2, 5, 4])
        sinkb = place("sink", [P, C_HEADS])
        eps = place("eps", [P, 1])
        ident = ident_t[:, 0:P]
        not_first = ident_t[:, P:P + 1]
        OF = place("o_mlp", [P, KT, TOK], at=U_AT)

        def region(*items):
            got, at = [], M0
            for name, shape, off in items:
                at = M0 + off if off is not None else at
                n = 4 * math.prod(shape[1:])
                assert at + n <= M_END, name
                got.append(place(name, shape, at=at))
                at += n
            return got

        OM, R1, R2, TC = region(("o_mixer", [P, KT, TOK], 0), ("rstd_o", [P, TOK], None),
                                ("rstd_h", [P, TOK], None), ("normed", [P, KT, TOK], None))
        (QK, KD, VT, RT, RC, SM, PB, PT, XR, PR) = region(
            ("qkv", [P, 12, TOK], 0), ("k_dup", [P, C_KV, TOK], None), ("v_tok", [P, 4, 2 * P], None),
            ("rope_tmp", [P, 2, TOK], None), ("rope_tab", [P, ROPE_COLS], None), ("scores", [P, 2, TOK], None),
            ("probs", [P, 2, 3, TOK], None), ("probs_t", [P, 2, 3, TOK], None),
            ("x_rows", [P, 4, D], 4 * (26 * TOK + ROPE_COLS)), ("par_rows", [P, NPAR, P], None))
        (X0, XV, BF, DF, HS, HD, DC, W4, FWT, FBI) = region(
            ("x0", [P, KT, TOK], 0), ("x1v", [P, KT, TOK], None), ("filter_spec", [P, 5, D], None),
            ("dft", [P, 2, 6 * P], None), ("h_sum", [P, 2, D], None), ("h_diff", [P, 2, D], None),
            ("decay", [P, 2, D], None), ("f_w4", [P, D], None), ("f_w", [P, 4 * FW], None), ("f_b", [P, 3], None))
        YS, VX, IF = region(("y_spec", [P, 2, 4, 512], 4 * (16 * TOK + 5 * D + 12 * P)),
                            ("x1v_tok", [P, 2, 2, 512], None), ("idft", [P, 4, SEQ], None))
        FA = place("f_act", [P, 2, SEQ], at=SQ_AT)
        FT = place("f_arg", [P, 2, SEQ], at=SQ_AT + 8 * SEQ)
        VC = place("v_conv", [P, 2, TOK], at=MA_AT)
        cosT, sinT = RC[:, 0:TOK], RC[:, TOK:2 * TOK]

        def rope_mat(m):
            return RC[:, 2 * TOK + m * P:2 * TOK + (m + 1) * P]
        maskT = RC[:, 2 * TOK + 5 * P:ROPE_COLS].rearrange("p (b k) -> p b k", b=2)

        lo4 = es.enter_context(nc.psum_tensor("lo4", [P, 4, 512], F32))
        stat = es.enter_context(nc.psum_tensor("stat", [P, 512], F32))
        modp = es.enter_context(nc.psum_tensor("modp", [P, 512], F32))
        hi2 = es.enter_context(nc.psum_tensor("hi2", [P, 2, 512], F32))
        bank = [lo4[:, 0, :], lo4[:, 1, :], lo4[:, 2, :], lo4[:, 3, :], stat[:, :], modp[:, :], hi2[:, 0, :], hi2[:, 1, :]]

        raw_in = [sem("raw_in0"), sem("raw_in1")]
        hi_ready, lo_ready, tile_done = sem("hi_ready"), sem("lo_ready"), sem("tile_done")
        mod_in = [sem("mod_in0"), sem("mod_in1")]
        mod_step, mod_reduced, mod_final = sem("mod_step"), sem("mod_reduced"), sem("mod_final")
        rows_in, rows_clear, const_in, x_in, tab_in = (sem("rows_in"), sem("rows_clear"), sem("const_in"),
                                                       sem("x_in"), sem("tab_in"))
        start_in = sem("start_in")
        consts_set, par_turned, par_ready, silu_ready = (sem("consts_set"), sem("par_turned"), sem("par_ready"),
                                                         sem("silu_ready"))
        x_turned, h_loaded = sem("x_turned"), sem("h_loaded")
        sq_ready, stat_step, root_ready, rstd_ready = (sem("sq_ready"), sem("stat_step"), sem("root_ready"),
                                                       sem("rstd_ready"))
        on_dve, on_pool, h_ready = sem("on_dve"), sem("on_pool"), sem("h_ready")
        hn_dve, hn_pool, uf_ready, uh_ready, u_ready = (sem("hn_dve"), sem("hn_pool"), sem("uf_ready"),
                                                        sem("uh_ready"), sem("u_ready"))
        o_ready = sem("o_ready")
        tap0, tap1, conv_done, silu_done = sem("tap0"), sem("tap1"), sem("conv_done"), sem("silu_done")
        mf_ready, mh_ready, ml_ready = sem("mf_ready"), sem("mh_ready"), sem("ml_ready")
        out_turned, out_copied, out_stored = sem("out_turned"), sem("out_copied"), sem("out_stored")
        q_evac, q_sq, q_turned, q_root, q_cos, q_roped = (sem("q_evac"), sem("q_sq"), sem("q_turned"), sem("q_root"),
                                                          sem("q_cos"), sem("q_roped"))
        v_turned, v_ready = sem("v_turned"), sem("v_ready")
        s_ready, s_masked, s_max, s_exp, s_norm = (sem("s_ready"), sem("s_masked"), sem("s_max"), sem("s_exp"),
                                                   sem("s_norm"))
        p_turned, p_ev_lat, p_ev_ctx, pv_done, ao_hi, ao_lo = (sem("p_turned"), sem("p_ev_lat"), sem("p_ev_ctx"),
                                                               sem("pv_done"), sem("ao_hi"), sem("ao_lo"))
        z_evac, z_tap, z_conv = sem("z_evac"), sem("z_tap"), sem("z_conv")
        f_mm, f_arg, f_sin, f_h, f_spec, f_sev = (sem("f_mm"), sem("f_arg"), sem("f_sin"), sem("f_h"), sem("f_spec"),
                                                  sem("f_sev"))
        c_turned, c_vt_act, c_vt_dve, c_fwd, c_prod, c_y = (sem("c_turned"), sem("c_vt_act"), sem("c_vt_dve"),
                                                            sem("c_fwd"), sem("c_prod"), sem("c_y"))
        c_inv, c_skip, c_gated, c_hi, c_lo = sem("c_inv"), sem("c_skip"), sem("c_gated"), sem("c_hi"), sem("c_lo")
        dve_chain = sem("dve_chain")

        NL = [TOK if i < DEPTH - 1 else SEQ for i in range(DEPTH)]

        def col(name, r, n=1):
            return par[:, ROW0[name] + r:ROW0[name] + r + n]

        ATT = [i for i in range(DEPTH) if KIND[i] != 1]
        EV = {i: 12 if KIND[i] == 0 else 10 for i in ATT}
        HEADS = {i: A_HEADS if KIND[i] == 0 else C_HEADS for i in ATT}
        VCH = {i: 2 if KIND[i] == 0 else 1 for i in ATT}

        def ahead(per, i):
            return sum(per[j] for j in ATT if j < i)

        def turns_ahead(i):
            return 10 * len([j for j in ATT if j < i])

        def norms_ahead(i):
            return 10 * len([j for j in ATT if j < i and KIND[j] == 0])

        PAIRS = []
        for i in range(DEPTH):
            PAIRS += [("in", i, t) for t in range(12 if KIND[i] == 1 else 6)]
            PAIRS += [("out", i, t) for t in range(4)]
            PAIRS += [("up", i, t) for t in range(FM)]
            PAIRS += [("down", i, t) for t in range(4)]
        PAIR0 = {(ph, i): q for q, (ph, i, t) in enumerate(PAIRS) if t == 0}

        def released(q):
            ph, i, t = PAIRS[q]
            if ph == "in" and KIND[i] == 0:
                return q_evac, ahead(EV, i) + 2 * t + 2
            if ph == "in" and KIND[i] == 2:
                return q_evac, ahead(EV, i) + (2 * t + 2 if t < 4 else t + 5)
            if ph == "in":
                return z_evac, 2 * t + 2
            if ph == "out":
                return o_ready, 2 * i * KT + 2 * t + 2
            if ph == "down":
                return o_ready, (2 * i + 1) * KT + 2 * t + 2
            return (conv_done, i * FM + t + 2) if t % 2 == 0 else (mf_ready, i * FM + t + 1)

        def mods_at(n):
            for i in range(DEPTH - 1):
                k = 2 * MB * (i + 1)
                t = n - FIRST["out", i]
                if 0 <= t < 3:
                    return [k + 2 * t, k + 2 * t + 1]
                t = n - FIRST["up", i]
                if 0 <= t < FM:
                    return [k + 6 + t]
                t = n - FIRST["down", i]
                if 0 <= t < 10:
                    return [k + 6 + FM + 2 * t, k + 7 + FM + 2 * t]
            return []

        block = es.enter_context(nc.Block())

        @block.sync
        def _(sp):
            sp.wait_ge(rows_clear, 1)
            for name, k in ROWS:
                src = a[name]
                flat = src.rearrange({1: "(r q) -> r q", 2: "a (r q) -> (a r) q",
                                      3: "a b (r q) -> (a b r) q"}[len(src.shape)], q=P)
                r = 0
                while r < k:
                    g = ROW0[name] + r
                    m = min(k - r, P - g % P)
                    sp.dma_start(PR[g % P:g % P + m, g // P, :], flat[r:r + m, :]).then_inc(rows_in, 16)
                    r += m
            sp.dma_start(ident_t[:, :], a["k_ident"]).then_inc(const_in, 16)

            def raw(n):
                if n >= NT:
                    return
                name, j, r0, nr, c0, w = TILES[n]
                if n >= 2:
                    sp.wait_ge(lo_ready, n - 1)
                src = a[name][j, r0 * P:(r0 + nr) * P, c0:c0 + w].rearrange("(k p) n -> p k n", p=P)
                sp.dma_start(RAW[:, n % 2, 0:nr * w].rearrange("p (k n) -> p k n", n=w),
                             src).then_inc(raw_in[n % 2], 16)

            def mod(k):
                layer, r = divmod(k, 2 * MB)
                if k >= 2:
                    sp.wait_ge(mod_step, 8 * (k - 1))
                src = a["mod_w"][layer, (r % 2) * 4 * P:(r % 2) * 4 * P + 4 * P, (r // 2) * TW:(r // 2) * TW + TW]
                sp.dma_start(MR[:, k % 2, :, :], src.rearrange("(k p) n -> p k n", p=P)).then_inc(mod_in[k % 2], 16)

            mod(0)
            mod(1)
            for t in range(4):
                src = a["x"] if t < 2 else a["ctx"]
                sp.dma_start(XR[:, t, :], src[0, (t % 2) * P:(t % 2) * P + P, :]).then_inc(x_in, 16)
            sp.dma_start(RC[:, 0:2 * TOK + P], a["k_rope_a"]).then_inc(start_in, 16)
            sp.dma_start(sinkb[:, :], a["c_sink"].broadcast_to([P, C_HEADS])).then_inc(start_in, 16)
            raw(0)
            raw(1)
            for k in range(2, 2 * MB + 2):
                mod(k)
            raw(2)
            raw(3)
            k = 2 * MB + 2
            for n in range(NT):
                raw(n + 4)
                for _m in mods_at(n):
                    if k < 2 * MB * DEPTH:
                        mod(k)
                        k += 1

            for t in range(2):
                sp.wait_ge(out_copied, 2 * t + 2)
                sp.dma_start(out[0, t * P:t * P + P, :], XR[:, t, :]).then_inc(out_stored, 16)
            sp.wait_ge(out_stored, 32)

        @block.tensor
        def _(pe):
            mm = nc.tensor.matmul

            def reduce_mod(k):
                layer, r = divmod(k, 2 * MB)
                if r == 0 and layer > 0:
                    pe.wait_ge(mod_final, layer)
                pe.wait_ge(mod_step, 8 * (k + 1))
                for v in range(2):
                    for cc in range(2):
                        at = v * NMOD * KT + (r // 2) * 2 + cc
                        last = mm(modp[:, at:at + 1], MA[:, k % 2, v, cc * P:(cc + 1) * P], ones[:, 0:1],
                                  start=(r % 2 == 0 and v == 0 and cc == 0), stop=(r % 2 == 1), skip_group_check=True)
                last.then_inc(mod_reduced, 1)

            def tile(n, q, N, hi, lo, first, last, kt0=0, arrive=None, fresh=False):
                nr, w = TILES[n][3], TILES[n][5]
                b0 = 2 * (q % 2)
                if first and q >= 2:
                    pe.wait_ge(*released(q - 2))
                pe.wait_ge(lo_ready, n + 1)
                h3 = WH[:, n % 2, 0:nr * w].rearrange("p (k n) -> p k n", n=w)
                l3 = WL[:, n % 2, 0:nr * w].rearrange("p (k n) -> p k n", n=w)
                for k in range(nr):
                    if arrive:
                        arrive(kt0 + k)
                    for m in range(w // P):
                        o = bank[b0 + m][:, 0:N]
                        c = slice(m * P, (m + 1) * P)
                        x, y = hi[:, kt0 + k, 0:N], lo[:, kt0 + k, 0:N]
                        mm(o, h3[:, k, c], x, start=(first and k == 0), stop=False)
                        mm(o, h3[:, k, c], y, start=False, stop=False)
                        ins = mm(o, l3[:, k, c], x, start=False, stop=(last and k == nr - 1))
                    if k == nr // 2 - 1:
                        for x in mods_at(n - 2)[-1:] if not fresh else []:
                            reduce_mod(x)
                ins.then_inc(tile_done, 1)

            def end_mods(n):
                for x in mods_at(n - 1)[:-1]:
                    reduce_mod(x)

            def stat_chunk(seq, c, N):
                s = seq * KT + c
                if c == 0 and seq > 0:
                    pe.wait_ge(root_ready, seq)
                pe.wait_ge(sq_ready, s + 1)
                mm(bank[4][:, 0:N], ones[:, :], SQ[:, s % 2, 0:N], start=(c == 0), stop=(c == KT - 1)).then_inc(stat_step, 1)

            pe.wait_ge(const_in, 16)
            pe.wait_ge(rows_in, 16 * N_ROW_DMAS)
            for t in range(NPAR):
                last = nc.tensor.transpose(bank[6 + t // 4][:, (t % 4) * P:(t % 4 + 1) * P], PR[:, t, :], ident)
            last.then_inc(par_turned, 1)
            pe.wait_ge(x_in, 64)
            for c in range(KT):
                if c >= 4:
                    pe.wait_ge(h_loaded, c - 3)
                for t in range(4):
                    last = nc.tensor.transpose(bank[c % 4][:, t * P:(t + 1) * P], XR[:, t, c * P:(c + 1) * P], ident)
                last.then_inc(x_turned, 1)
            pe.wait_ge(consts_set, 1)
            for k in range(2 * MB):
                reduce_mod(k)

            def turn_q(i, r):
                g = turns_ahead(i) + r
                N = NL[i] if r < 8 else TOK
                if r >= 2:
                    pe.wait_ge(q_roped, g - 1)
                if r == 0:
                    pe.wait_ge(mod_final, i + 1)
                    pe.wait_ge(*((tab_in, TAB_AT[i]) if i else (start_in, 32)))
                if KIND[i] == 0:
                    pe.wait_ge(q_evac, ahead(EV, i) + r + 1)
                    mm(bank[4 + r % 2][:, 0:N], ones[:, :], SQ[:, r % 2, 0:N], start=True, stop=True)
                    mm(bank[6 + r % 2][:, 0:N], rope_mat(0), QK[:, r, 0:N], start=True, stop=True).then_inc(q_turned, 1)
                elif r < 8:
                    pe.wait_ge(q_evac, ahead(EV, i) + r + 1)
                    mm(bank[6 + r % 2][:, 0:N], rope_mat(0), QK[:, r, 0:N], start=True, stop=True).then_inc(q_turned, 1)
                else:
                    pe.wait_ge(q_evac, ahead(EV, i) + 9)
                    mm(bank[4 + r % 2], rope_mat(1 + 2 * (r - 8)), QK[:, 8, :], start=True, stop=True)
                    mm(bank[6 + r % 2], rope_mat(2 + 2 * (r - 8)), QK[:, 8, :], start=True, stop=True).then_inc(q_turned, 1)

            def turn_v(i, j):
                pe.wait_ge(q_evac, ahead(EV, i) + EV[i] - VCH[i] + j + 1)
                pe.wait_ge(q_roped, turns_ahead(i) + 9 + j)
                src = QK[:, EV[i] - VCH[i] + j, :]
                for t in range(4):
                    last = nc.tensor.transpose(bank[4 + j][:, t * P:(t + 1) * P], src[:, t * P:(t + 1) * P], ident)
                last.then_inc(v_turned, 1)

            def attention(i):
                G, A = ahead(HEADS, i), KIND[i] == 0
                ctx = NL[i] == TOK
                part = A_HEADS // A_KV if A else C_HEADS // C_KV

                def scores(h):
                    g = G + h
                    if h == 0:
                        pe.wait_ge(q_roped, turns_ahead(i) + 10)
                        pe.wait_ge(v_ready, ahead(VCH, i) + VCH[i])
                    else:
                        pe.wait_ge(*((s_exp, g) if A else (s_masked, MASKED(i) + h)))
                    if A:
                        q, k = QK[:, h, :], QK[:, 8 + h // part, :]
                    else:
                        ps = slice(64 * (h % 2), 64 * (h % 2) + 64)
                        q, k = QK[ps, h // 2, :], KD[ps, h // part, :]
                    for b in range(2):
                        last = mm(bank[6 + b], q[:, b * P:(b + 1) * P], k[:, 0:TOK], start=True, stop=True)
                    if ctx:
                        if h > 0:
                            pe.wait_ge(s_exp, g)
                        for b in range(2):
                            last = mm(bank[4][:, b * CTX:(b + 1) * CTX], q[:, SEQ + b * P:SEQ + (b + 1) * P],
                                      k[:, SEQ:TOK], start=True, stop=True)
                    last.then_inc(s_ready, 1)

                def turn(h):
                    g = G + h
                    pe.wait_ge(s_norm, g + 1)
                    if h == 0:
                        pe.wait_ge(*released(PAIR0["out", i] - 2))
                        pe.wait_ge(*released(PAIR0["out", i] - 1))
                    else:
                        pe.wait_ge(p_ev_lat, g)
                        if ctx:
                            pe.wait_ge(p_ev_ctx, CTXG(i) + h)
                    for kt in range(4):
                        for b in range(2):
                            last = nc.tensor.transpose(bank[kt // 2][:, (kt % 2) * SEQ + b * P:(kt % 2) * SEQ + (b + 1) * P],
                                                       PB[:, h % 2, b, kt * P:(kt + 1) * P], ident)
                    if ctx:
                        for kt in range(2):
                            for b in range(2):
                                last = nc.tensor.transpose(bank[2][:, kt * CTX + b * P:kt * CTX + (b + 1) * P],
                                                           PB[:, h % 2, 2, b * CTX + kt * P:b * CTX + (kt + 1) * P], ident)
                    last.then_inc(p_turned, 1)

                def pv(h):
                    g = G + h
                    if h > 0:
                        pe.wait_ge(ao_lo, g)
                    vc = (h // part) * P
                    pe.wait_ge(p_ev_lat, g + 1)
                    for kt in range(4):
                        last = mm(bank[3][:, 0:SEQ], VT[:, kt, vc:vc + P], PT[:, h % 2, kt // 2, (kt % 2) * SEQ:(kt % 2 + 1) * SEQ],
                                  start=(kt == 0), stop=(kt == 3))
                    if ctx:
                        pe.wait_ge(p_ev_ctx, CTXG(i) + h + 1)
                        for kt in range(2):
                            last = mm(bank[3][:, SEQ:TOK], VT[:, 2 + kt, vc:vc + P], PT[:, h % 2, 2, kt * CTX:(kt + 1) * CTX],
                                      start=(kt == 0), stop=(kt == 1))
                    last.then_inc(pv_done, 1)

                scores(0)
                for h in range(HEADS[i]):
                    if h + 1 < HEADS[i]:
                        scores(h + 1)
                    turn(h)
                    if h > 0:
                        pv(h - 1)
                pv(HEADS[i] - 1)

            def filter_stage(t):
                if t < 3:
                    if t == 0:
                        pe.wait_ge(tab_in, TAB_AT[1])
                        pe.wait_ge(mod_final, 2)
                        mm(bank[6][0:FW, 0:SEQ], FWT[0:FEMB, 0:FW], FA[0:FEMB, 0, :], start=True, stop=True).then_inc(f_mm, 1)
                    else:
                        pe.wait_ge(f_sin, t)
                        w = FW if t == 1 else 2 * FW
                        mm(bank[6][0:w, 0:SEQ], FWT[0:FW, t * FW:t * FW + w], FA[0:FW, t % 2, :], start=True,
                           stop=True).then_inc(f_mm, 1)
                elif t < 7:
                    tt, hf = divmod(t - 3, 2)
                    pe.wait_ge(f_sin, 3)
                    if t > 3:
                        pe.wait_ge(f_h, t - 3)
                    for d in range(2):
                        ps = slice(FW * d, FW * d + FW)
                        last = mm(bank[6 + d], FA[ps, 1, tt * P:(tt + 1) * P], W4[ps, hf * 512:(hf + 1) * 512],
                                  start=True, stop=True)
                    last.then_inc(f_mm, 1)
                else:
                    pe.wait_ge(f_h, 4)
                    for x in range(2 * (t - 7), 2 * (t - 7) + 2):
                        j, hf = divmod(x, 2)
                        if x >= 2:
                            pe.wait_ge(f_sev, x - 1)
                        src = HD if j in (2, 3) else HS
                        blk = (0, 1, 5, 3, 4)[j]
                        for kt in range(2):
                            last = mm(bank[6 + x % 2], DF[:, kt, blk * P:(blk + 1) * P], src[:, kt, hf * 512:(hf + 1) * 512],
                                      start=(kt == 0), stop=(kt == 1))
                        last.then_inc(f_spec, 1)

            def long_conv():
                def turn(w):
                    hf, st = divmod(w, 2)
                    if w == 0:
                        pe.wait_ge(z_conv, 3 * KT)
                        pe.wait_ge(root_ready, 3)
                    else:
                        pe.wait_ge(c_vt_act, w)
                        pe.wait_ge(c_vt_dve, w)
                    for tt in range(2):
                        for c in range(4):
                            last = nc.tensor.transpose(bank[4 + tt][:, c * P:(c + 1) * P],
                                                       XV[:, 4 * hf + c, st * SEQ + tt * P:st * SEQ + (tt + 1) * P], ident)
                    last.then_inc(c_turned, 1)

                def forward(w):
                    pe.wait_ge(c_vt_act, w + 1)
                    pe.wait_ge(c_vt_dve, w + 1)
                    if w == 0:
                        pe.wait_ge(*released(PAIR0["out", 1] - 1))
                    else:
                        pe.wait_ge(c_prod, 8 * w)
                    for j in range(4):
                        for tt in range(2):
                            last = mm(bank[j], DF[:, tt, j * P:(j + 1) * P], VX[:, w % 2, tt, :],
                                      start=(tt == 0), stop=(tt == 1))
                    last.then_inc(c_fwd, 1)

                def inverse(w):
                    pe.wait_ge(c_y, 4 * (w + 1))
                    if w == 0:
                        pe.wait_ge(tab_in, TAB_AT[1] + 16)
                        pe.wait_ge(f_sev, 10)
                    else:
                        pe.wait_ge(c_skip, 4 * w)
                    for c in range(4):
                        for j in range(4):
                            last = mm(bank[6 + c // 2][:, (c % 2) * SEQ:(c % 2 + 1) * SEQ], YS[:, w % 2, j, c * P:(c + 1) * P],
                                      IF[:, j, :], start=(j == 0), stop=(j == 3))
                    last.then_inc(c_inv, 1)

                turn(0)
                forward(0)
                turn(1)
                for w in range(4):
                    if w < 3:
                        forward(w + 1)
                    inverse(w)
                    if w < 2:
                        turn(w + 2)

            for i in range(DEPTH):
                N = NL[i]
                for c in range(KT):
                    stat_chunk(4 * i, c, TOK)
                n0, q0 = FIRST["in", i], PAIR0["in", i]
                if KIND[i] == 1:
                    for t in range(12):
                        tile(n0 + t, q0 + t, TOK, UH, UL, True, True,
                             arrive=(lambda k, b=2 * i * KT: pe.wait_ge(u_ready, b + k + 1)) if t == 0 else None,
                             fresh=True)
                        filter_stage(t)
                    long_conv()
                    arrive = lambda k: pe.wait_ge(c_lo, 8 * (k // 4 + 1))
                else:
                    for t in range(6):
                        nt = TOK if t >= 4 else N
                        tile(n0 + t, q0 + t, nt, UH, UL, True, True,
                             arrive=(lambda k, b=2 * i * KT: pe.wait_ge(u_ready, b + k + 1)) if t == 0 else None,
                             fresh=True)
                        if t > 0:
                            turn_q(i, 2 * t - 2)
                            turn_q(i, 2 * t - 1)
                    for j in range(VCH[i]):
                        turn_v(i, j)
                    attention(i)
                    G, per = ahead(HEADS, i), HEADS[i] // KT
                    arrive = lambda k, G=G, per=per: pe.wait_ge(ao_lo, G + per * (k + 1))
                n0, q0 = FIRST["out", i], PAIR0["out", i]
                for t in range(4):
                    tile(n0 + t, q0 + t, N, UH, UL, True, True, arrive=arrive if t == 0 else None)
                    end_mods(n0 + t)
                    if t > 0:
                        stat_chunk(4 * i + 1, 2 * t - 2, N)
                        stat_chunk(4 * i + 1, 2 * t - 1, N)
                stat_chunk(4 * i + 1, 6, N)
                stat_chunk(4 * i + 1, 7, N)
                for c in range(KT):
                    stat_chunk(4 * i + 2, c, N)
                n0, q0 = FIRST["up", i], PAIR0["up", i]
                for t in range(FM):
                    tile(n0 + t, q0 + t, N, UH, UL, True, True,
                         arrive=(lambda k, b=(2 * i + 1) * KT: pe.wait_ge(u_ready, b + k + 1)) if t == 0 else None)
                    end_mods(n0 + t)
                n0, q0 = FIRST["down", i], PAIR0["down", i]
                for t in range(12):
                    pair, third = divmod(t, 3)
                    n = n0 + t
                    tile(n, q0 + pair, N, MH, ML, third == 0, third == 2, kt0=8 * third,
                         arrive=(lambda k, b=i * FM: pe.wait_ge(ml_ready, b + k + 1)) if pair == 0 else None)
                    end_mods(n)
                    if third == 0 and pair > 0:
                        stat_chunk(4 * i + 3, 2 * pair - 2, N)
                        stat_chunk(4 * i + 3, 2 * pair - 1, N)
                stat_chunk(4 * i + 3, 6, N)
                stat_chunk(4 * i + 3, 7, N)

            for x in range(4):
                t, g = divmod(x, 2)
                for c in range(4):
                    if t == 0:
                        pe.wait_ge(h_ready, (2 * DEPTH - 1) * KT + 4 * g + c + 1)
                    last = nc.tensor.transpose(bank[x][:, c * P:(c + 1) * P], H[:, 4 * g + c, t * P:(t + 1) * P], ident)
                last.then_inc(out_turned, 1)

        @block.scalar
        def _(act):
            f = nc.scalar.activation

            def hi(n):
                if n >= NT:
                    return
                words = TILES[n][3] * TILES[n][5]
                act.wait_ge(raw_in[n % 2], 16 * (n // 2 + 1))
                if n >= 2:
                    act.wait_ge(tile_done, n - 1)
                f(WH[:, n % 2, 0:words], RAW[:, n % 2, 0:words], ACT.Copy).then_inc(hi_ready, 1)

            def square(seq, c, src, N, **kw):
                s = seq * KT + c
                if s >= 2:
                    act.wait_ge(stat_step, s - 1)
                f(SQ[:, s % 2, 0:N], src, ACT.Square, **kw).then_inc(sq_ready, 1)

            def root(seq, dst, N):
                act.wait_ge(stat_step, KT * (seq + 1))
                f(dst[:, 0:N], bank[4][:, 0:N], ACT.Sqrt, scale=1.0 / D, bias=eps[:, :]).then_inc(root_ready, 1)

            def pre_norm(i, w, N):
                seq, k = 4 * i + 2 * w, 2 * i + w
                for c in range(KT):
                    if k == 0:
                        act.wait_ge(h_loaded, c + 1)
                    else:
                        act.wait_ge(h_ready, (k - 1) * KT + c + 1)
                    square(seq, c, H[:, c, 0:N], N)
                root(seq, R2, N)
                for c in range(KT):
                    act.wait_ge(uf_ready, k * KT + c + 1)
                    f(UH[:, c, 0:N], TC[:, c, 0:N], ACT.Copy).then_inc(uh_ready, 1)

            def o_chunks(seq, t, q, dst, N, bias):
                for m in range(2):
                    c = 2 * t + m
                    src = bank[2 * (q % 2) + m][:, 0:N]
                    if bias:
                        square(seq, c, src, N, bias=col(bias, c))
                        f(dst[:, c, 0:N], src, ACT.Identity, bias=col(bias, c)).then_inc(o_ready, 1)
                    else:
                        square(seq, c, src, N)
                        f(dst[:, c, 0:N], src, ACT.Copy).then_inc(o_ready, 1)

            act.wait_ge(par_ready, 2)
            act.wait_ge(consts_set, 1)
            f(S2[:, 0, :], col("c", 0, KT), ACT.Silu)
            f(S2[:, 1, :], col("c_ctx", 0, KT), ACT.Silu).then_inc(silu_ready, 1)
            for c in range(KT):
                act.wait_ge(x_turned, c + 1)
                f(H[:, c, :], bank[c % 4], ACT.Copy).then_inc(h_loaded, 1)
            hi(0)
            hi(1)

            def attention_in(i):
                n0, q0, A = FIRST["in", i], PAIR0["in", i], KIND[i] == 0
                E = ahead(EV, i)

                def q_roots(t):
                    for r in (2 * t, 2 * t + 1):
                        g, gn = turns_ahead(i) + r, norms_ahead(i) + r
                        N = NL[i] if r < 8 else TOK
                        act.wait_ge(q_turned, g + 1)
                        if r >= 2:
                            act.wait_ge(q_roped, g - 1)
                        f(CV[:, r % 2, 0:N], bank[4 + r % 2][:, 0:N], ACT.Sqrt, scale=1.0 / A_DH,
                          bias=eps[:, :]).then_inc(q_root, 1)

                for t in range(6):
                    act.wait_ge(tile_done, n0 + t + 1)
                    hi(n0 + t + 2)
                    b0 = 2 * ((q0 + t) % 2)
                    if A:
                        for m in range(2):
                            c = 2 * t + m
                            N = NL[i] if c < 8 else TOK
                            src = bank[b0 + m][:, 0:N]
                            if c < 10:
                                if c >= 2:
                                    act.wait_ge(q_turned, turns_ahead(i) + c - 1)
                                f(SQ[:, c % 2, 0:N], src, ACT.Square)
                                gain = col("a_q_gain" if c < 8 else "a_k_gain", i // 3)
                                f(QK[:, c, 0:N], src, ACT.Copy, scale=gain).then_inc(q_evac, 1)
                            else:
                                f(QK[:, c, :], src, ACT.Copy).then_inc(q_evac, 1)
                        if t > 0 and t < 6:
                            q_roots(t - 1)
                    else:
                        for m in range(2 if t < 4 else 1):
                            c = 2 * t + m if t < 4 else t + 4
                            f(QK[:, c, :], bank[b0 + m], ACT.Identity, bias=col("c_b_qkv", c)).then_inc(q_evac, 1)

            def attention(i):
                G, A = ahead(HEADS, i), KIND[i] == 0
                ctx = NL[i] == TOK
                scale = (A_DH if A else C_DH) ** -0.5
                nE = 4 if ctx else 2

                def exps(h):
                    g, sl = G + h, small[:, h % 2, :, :]
                    act.wait_ge(s_max, g + 1)
                    if h >= 2:
                        act.wait_ge(p_turned, g - 1)
                    for b in range(nE):
                        nm, acc = sl[:, 1, b:b + 1], sl[:, 2, b:b + 1]
                        if b < 2:
                            dst = PB[:, h % 2, b, :]
                            src, sc = (bank[6 + b], scale) if A else (SM[:, b, :], 1.0)
                        else:
                            dst = PB[:, h % 2, 2, (b - 2) * CTX:(b - 1) * CTX]
                            src, sc = bank[4][:, (b - 2) * CTX:(b - 1) * CTX], scale
                        last = f(dst, src, ACT.Exp, scale=sc, bias=nm, accum_out=acc)
                    if not A:
                        last = f(sl[:, 4, 0:nE], sl[:, 1, 0:nE], ACT.Exp, bias=sinkb[:, h:h + 1])
                    last.then_inc(s_exp, 1)

                def evac(h):
                    g = G + h
                    act.wait_ge(p_turned, g + 1)
                    if h > 1:
                        act.wait_ge(pv_done, g - 1)
                    f(PT[:, h % 2, 0:2, :], lo4[:, 0:2, :], ACT.Copy).then_inc(p_ev_lat, 1)

                def o_hi(h):
                    g, N = G + h, NL[i]
                    act.wait_ge(pv_done, g + 1)
                    if A:
                        f(UH[:, h, 0:N], bank[3][:, 0:N], ACT.Copy).then_inc(ao_hi, 1)
                    else:
                        ps = slice(64 * (h % 2), 64 * (h % 2) + 64)
                        f(UH[ps, h // 2, 0:N], bank[3][ps, 0:N], ACT.Copy).then_inc(ao_hi, 1)

                exps(0)
                for h in range(HEADS[i]):
                    evac(h)
                    if h + 1 < HEADS[i]:
                        exps(h + 1)
                    if h > 0:
                        o_hi(h - 1)
                o_hi(HEADS[i] - 1)

            def hyena_in():
                n0, q0 = FIRST["in", 1], PAIR0["in", 1]
                for t in range(12):
                    act.wait_ge(tile_done, n0 + t + 1)
                    hi(n0 + t + 2)
                    for m in range(2):
                        c = 2 * t + m
                        if t < 4:
                            cm, dst = c, X0[:, c, :]
                        else:
                            s, isv = divmod(t - 4, 2)
                            cm = (8 + 8 * isv) + 2 * s + m
                            dst = VC[:, m, :] if isv else XV[:, 2 * s + m, :]
                        if c >= 2:
                            act.wait_ge(z_conv, c - 1)
                        f(CV[:, m, :], bank[2 * ((q0 + t) % 2) + m], ACT.Identity, bias=col("b_b_in", cm)).then_inc(z_evac, 1)
                        act.wait_ge(z_evac, c + 1)
                        f(dst, CV[:, m, :], ACT.Identity, scale=col("b_conv_w", 3 * KT + cm),
                          bias=col("b_conv_b", cm)).then_inc(z_tap, 1)
                    if t < 3:
                        act.wait_ge(f_arg, t + 1)
                        w = FW if t < 2 else 2 * FW
                        f(FA[0:w, (t + 1) % 2, :], FT[0:w, 0, :], ACT.Sin).then_inc(f_sin, 1)
                    elif t >= 7:
                        for x in range(2 * (t - 7), 2 * (t - 7) + 2):
                            j, hf = divmod(x, 2)
                            act.wait_ge(f_spec, x + 1)
                            f(BF[:, j, hf * 512:(hf + 1) * 512], bank[6 + x % 2], ACT.Copy).then_inc(f_sev, 1)

            def long_conv():
                def vt(w):
                    act.wait_ge(c_turned, w + 1)
                    if w >= 2:
                        act.wait_ge(c_fwd, w - 1)
                    f(VX[:, w % 2, 0, :], bank[4], ACT.Copy).then_inc(c_vt_act, 1)

                def part(w):
                    hf, st = divmod(w, 2)
                    for c in range(4):
                        act.wait_ge(c_gated, 4 * w + c + 1)
                        f(UH[:, 4 * hf + c, st * SEQ:(st + 1) * SEQ], XV[:, 4 * hf + c, st * SEQ:(st + 1) * SEQ],
                          ACT.Copy).then_inc(c_hi, 1)

                vt(0)
                vt(1)
                for w in range(4):
                    if w < 2:
                        part(w)
                        vt(w + 2)
                    else:
                        part(w)

            for i in range(DEPTH):
                N = NL[i]
                pre_norm(i, 0, TOK)
                if KIND[i] == 1:
                    hyena_in()
                    long_conv()
                else:
                    attention_in(i)
                    attention(i)
                n0, q0 = FIRST["out", i], PAIR0["out", i]
                for t in range(4):
                    act.wait_ge(tile_done, n0 + t + 1)
                    hi(n0 + t + 2)
                    o_chunks(4 * i + 1, t, q0 + t, OM, N, (None, "b_b_out", "c_b_out")[KIND[i]])
                root(4 * i + 1, R1, N)
                pre_norm(i, 1, N)
                n0, q0 = FIRST["up", i], PAIR0["up", i]
                for s in range(FM // 2):
                    g = n0 + 2 * s
                    act.wait_ge(tile_done, g + 1)
                    hi(g + 2)
                    for m in range(2):
                        c = 2 * s + m
                        if c >= 2:
                            act.wait_ge(ml_ready, i * FM + c - 1)
                        f(CV[:, m, 0:N], bank[2 * ((q0 + 2 * s) % 2) + m][:, 0:N], ACT.Identity,
                          scale=col("ffn_conv_w", (3 * i + 1) * FM + c), bias=col("ffn_conv_b", i * FM + c)).then_inc(tap0, 1)
                    for m in range(2):
                        c = 2 * s + m
                        act.wait_ge(conv_done, i * FM + c + 1)
                        f(CV[:, m, 0:N], CV[:, m, 0:N], ACT.Silu).then_inc(silu_done, 1)
                    act.wait_ge(tile_done, g + 2)
                    hi(g + 3)
                    for m in range(2):
                        c = 2 * s + m
                        act.wait_ge(mf_ready, i * FM + c + 1)
                        f(MH[:, c, 0:N], CV[:, m, 0:N], ACT.Copy).then_inc(mh_ready, 1)
                n0, q0 = FIRST["down", i], PAIR0["down", i]
                for t in range(12):
                    pair, third = divmod(t, 3)
                    act.wait_ge(tile_done, n0 + t + 1)
                    hi(n0 + t + 2)
                    if third == 2:
                        o_chunks(4 * i + 3, pair, q0 + pair, OF, N, None)
                root(4 * i + 3, R1, N)

            for x in (1, 3):
                act.wait_ge(out_turned, x + 1)
                act.wait_ge(out_copied, x)
                f(XR[:, x // 2, 512:1024], bank[x], ACT.Copy).then_inc(out_copied, 1)

        @block.vector
        def _(dve):
            tt, ts, stt = nc.vector.tensor_tensor, nc.vector.tensor_scalar, nc.vector.scalar_tensor_tensor
            chained = [0]

            def link(ins):
                chained[0] += 1
                ins.then_inc(dve_chain, 1)
                dve.wait_ge(dve_chain, chained[0])

            def lo(n):
                if n >= NT:
                    return
                words = TILES[n][3] * TILES[n][5]
                dve.wait_ge(hi_ready, n + 1)
                tt(WL[:, n % 2, 0:words], RAW[:, n % 2, 0:words], WH[:, n % 2, 0:words].bitcast(F32),
                   ALU.subtract).then_inc(lo_ready, 1)

            def mod(k):
                dve.wait_ge(mod_in[k % 2], 16 * (k // 2 + 1))
                if k >= 2:
                    dve.wait_ge(mod_reduced, k - 1)
                for j in range(4):
                    for v in range(2):
                        s = S2[:, v, 4 * (k % 2) + j:4 * (k % 2) + j + 1]
                        acc = MA[:, k % 2, v, :]
                        if j == 0:
                            ts(acc, MR[:, k % 2, j, :], s, None, ALU.mult).then_inc(mod_step, 1)
                        else:
                            dve.wait_ge(mod_step, 8 * k + 2 * j + v - 1)
                            stt(acc, MR[:, k % 2, j, :], s, acc, ALU.mult, ALU.add).then_inc(mod_step, 1)

            def finish_mod(i):
                dve.wait_ge(mod_reduced, 2 * MB * (i + 1))
                W = NMOD * KT
                for v in range(2):
                    ins = tt(modv[:, v, :], modp[:, v * W:(v + 1) * W], col("mod_b", i * W, W), ALU.add)
                link(ins)
                for v in range(2):
                    g = [col("norm_g", (4 * i + n) * KT, KT) for n in range(4)]
                    m = [modv[:, v, j * KT:(j + 1) * KT] for j in range(NMOD)]
                    stt(coef[:, v, 0, :], m[1], 1.0, g[0], ALU.add, ALU.mult)
                    tt(coef[:, v, 1, :], m[2], g[1], ALU.mult)
                    stt(coef[:, v, 2, :], m[4], 1.0, g[2], ALU.add, ALU.mult)
                    ins = tt(coef[:, v, 3, :], m[5], g[3], ALU.mult)
                ins.then_inc(mod_final, 1)
                dve.wait_ge(mod_final, i + 1)

            def rstd(seq, r, N):
                dve.wait_ge(root_ready, seq + 1)
                nc.vector.reciprocal(r[:, 0:N], r[:, 0:N]).then_inc(rstd_ready, 1)
                dve.wait_ge(rstd_ready, seq + 1)

            def residual(i, w, O, N):
                k, seq = 2 * i + w, 4 * i + 2 * w + 1
                rstd(seq, R1, N)

                def normed(c):
                    tt(TC[:, c, 0:N], O[:, c, 0:N], R1[:, 0:N], ALU.mult).then_inc(on_dve, 1)

                normed(0)
                for c in range(KT):
                    if c % 2 == 0:
                        if c + 2 < KT:
                            normed(c + 2)
                        dve.wait_ge(on_dve, k * 4 + c // 2 + 1)
                    else:
                        dve.wait_ge(on_pool, k * 4 + c // 2 + 1)
                    for v in range(N // SEQ):
                        s = slice(v * SEQ, (v + 1) * SEQ)
                        ins = stt(H[:, c, s], TC[:, c, s], coef[:, v, 1 + 2 * w, c:c + 1], H[:, c, s], ALU.mult, ALU.add)
                    ins.then_inc(h_ready, 1)

            def pre_norm(i, w, N):
                k, seq = 2 * i + w, 4 * i + 2 * w
                rstd(seq, R2, N)

                def normed(c):
                    tt(TC[:, c, 0:N], H[:, c, 0:N], R2[:, 0:N], ALU.mult).then_inc(hn_dve, 1)

                def low(c):
                    dve.wait_ge(uh_ready, k * KT + c + 1)
                    tt(UL[:, c, 0:N], TC[:, c, 0:N], UH[:, c, 0:N].bitcast(F32), ALU.subtract).then_inc(u_ready, 1)

                normed(0)
                for c in range(KT):
                    if c % 2 == 0:
                        if c + 2 < KT:
                            normed(c + 2)
                        dve.wait_ge(hn_dve, k * 4 + c // 2 + 1)
                    else:
                        dve.wait_ge(hn_pool, k * 4 + c // 2 + 1)
                    for v in range(N // SEQ):
                        s = slice(v * SEQ, (v + 1) * SEQ)
                        ins = ts(TC[:, c, s], TC[:, c, s], coef[:, v, 2 * w, c:c + 1],
                                 modv[:, v, 3 * w * KT + c:3 * w * KT + c + 1], ALU.mult, ALU.add)
                    ins.then_inc(uf_ready, 1)
                    if c > 0:
                        low(c - 1)
                low(KT - 1)

            nc.vector.memset(eps[:, :], EPS)
            nc.vector.memset(ones[:, :], 1.0).then_inc(consts_set, 1)
            dve.wait_ge(par_turned, 1)
            nc.vector.tensor_copy(par[:, 0:512], bank[6])
            nc.vector.tensor_copy(par[:, 512:NPAR * P], bank[7][:, 0:NPAR * P - 512]).then_inc(par_ready, 2)
            dve.wait_ge(silu_ready, 1)
            dve.wait_ge(par_ready, 2)
            for k in range(2 * MB):
                mod(k)
            lo(0)
            lo(1)
            finish_mod(0)

            def rope(i, t):
                for r in (2 * t, 2 * t + 1):
                    g = turns_ahead(i) + r
                    N = NL[i] if r < 8 else TOK
                    turned = bank[6 + r % 2][:, 0:N]
                    tmp = RT[:, r % 2, 0:N]
                    if KIND[i] == 0:
                        dve.wait_ge(q_root, norms_ahead(i) + r + 1)
                        nc.vector.reciprocal(CV[:, r % 2, 0:N], CV[:, r % 2, 0:N])
                    dve.wait_ge(q_turned, g + 1)
                    link(tt(tmp, turned, sinT[:, 0:N], ALU.mult))
                    if KIND[i] == 0:
                        dve.wait_ge(q_cos, QCOS(i) + r + 1)
                        link(tt(tmp, tmp, QK[:, r, 0:N], ALU.add))
                        tt(QK[:, r, 0:N], tmp, CV[:, r % 2, 0:N], ALU.mult).then_inc(q_roped, 1)
                    elif r < 8:
                        dve.wait_ge(q_cos, QCOS(i) + r + 1)
                        tt(QK[:, r, 0:N], tmp, QK[:, r, 0:N], ALU.add).then_inc(q_roped, 1)
                    else:
                        link(tt(KD[:, r - 8, :], bank[4 + r % 2], cosT, ALU.mult))
                        tt(KD[:, r - 8, :], KD[:, r - 8, :], tmp, ALU.add).then_inc(q_roped, 1)

            def attention_in(i):
                n0 = FIRST["in", i]
                for t in range(6):
                    lo(n0 + t + 2)
                    if t == 0:
                        dve.wait_ge(*((tab_in, TAB_AT[i]) if i else (start_in, 32)))
                    if t > 0:
                        rope(i, t - 1)
                for j in range(VCH[i]):
                    dve.wait_ge(v_turned, ahead(VCH, i) + j + 1)
                    if KIND[i] == 0:
                        nc.vector.tensor_copy(VT[:, :, j * P:(j + 1) * P],
                                              bank[4 + j].rearrange("p (k d) -> p k d", k=4)).then_inc(v_ready, 1)
                    else:
                        src = bank[4].rearrange("p (k g d) -> p k g d", k=4, g=2)
                        dst = VT[:, :, :].rearrange("p k (g u d) -> p k g u d", g=2, u=2)
                        for u in range(2):
                            ins = nc.vector.tensor_copy(dst[:, :, :, u, :], src)
                        ins.then_inc(v_ready, 1)

            def attention(i):
                G, A = ahead(HEADS, i), KIND[i] == 0
                ctx = NL[i] == TOK
                scale = (A_DH if A else C_DH) ** -0.5
                nE = 4 if ctx else 2

                def maxima(h):
                    g, sl = G + h, small[:, h % 2, :, :]
                    dve.wait_ge(s_ready, g + 1)
                    if h >= 2 or (h and not A):
                        dve.wait_ge(s_exp, g - 1 if A else g)
                    if A:
                        ins = nc.vector.tensor_reduce(sl[:, 0, 0:2], hi2[:, :, :], AX.X, ALU.max)
                    else:
                        for b in range(2):
                            ins = nc.vector.tensor_tensor_reduce(SM[:, b, :], hi2[:, b, :], maskT[:, b, :], scale, -3e38,
                                                                 ALU.add, ALU.max, sl[:, 0, b:b + 1])
                        ins.then_inc(s_masked, 1)
                    if ctx:
                        ins = nc.vector.tensor_reduce(sl[:, 0, 2:4], bank[4].rearrange("p (b k) -> p b k", b=2), AX.X, ALU.max)
                    if A:
                        link(ins)
                        ts(sl[:, 1, 0:nE], sl[:, 0, 0:nE], -scale, None, ALU.mult).then_inc(s_max, 1)
                    else:
                        if ctx:
                            link(ins)
                            link(ts(sl[:, 0, 2:4], sl[:, 0, 2:4], scale, None, ALU.mult))
                        dve.wait_ge(s_masked, MASKED(i) + h + 1)
                        ts(sl[:, 1, 0:nE], sl[:, 0, 0:nE], sinkb[:, h:h + 1], -1.0, ALU.max, ALU.mult).then_inc(s_max, 1)

                def normalise(h):
                    g, sl = G + h, small[:, h % 2, :, :]
                    dve.wait_ge(s_exp, g + 1)
                    if not A:
                        link(tt(sl[:, 2, 0:nE], sl[:, 2, 0:nE], sl[:, 4, 0:nE], ALU.add))
                    link(nc.vector.reciprocal(sl[:, 3, 0:nE], sl[:, 2, 0:nE]))
                    for b in range(nE):
                        p = PB[:, h % 2, b, :] if b < 2 else PB[:, h % 2, 2, (b - 2) * CTX:(b - 1) * CTX]
                        ins = ts(p, p, sl[:, 3, b:b + 1], None, ALU.mult)
                    ins.then_inc(s_norm, 1)

                def evac(h):
                    g = G + h
                    if ctx:
                        dve.wait_ge(p_turned, g + 1)
                        if h > 1:
                            dve.wait_ge(pv_done, g - 1)
                        nc.vector.tensor_copy(PT[:, h % 2, 2, :], bank[2]).then_inc(p_ev_ctx, 1)

                def o_lo(h):
                    g, N = G + h, NL[i]
                    dve.wait_ge(ao_hi, g + 1)
                    ps, c = (slice(0, P), h) if A else (slice(64 * (h % 2), 64 * (h % 2) + 64), h // 2)
                    tt(UL[ps, c, 0:N], bank[3][ps, 0:N], UH[ps, c, 0:N].bitcast(F32), ALU.subtract).then_inc(ao_lo, 1)

                maxima(0)
                normalise(0)
                for h in range(HEADS[i]):
                    if h + 1 < HEADS[i]:
                        maxima(h + 1)
                    evac(h)
                    if h + 1 < HEADS[i]:
                        normalise(h + 1)
                    if h > 0:
                        o_lo(h - 1)
                o_lo(HEADS[i] - 1)

            def hyena_in():
                n0 = FIRST["in", 1]
                TWO_PI = 2.0 * math.pi
                C1 = 6.28125
                MAGIC = 1.5 * 2.0 ** 23
                for t in range(12):
                    lo(n0 + t + 2)
                    for m in range(2):
                        c = 2 * t + m
                        if t < 4:
                            cm, dst = c, X0[:, c, :]
                        else:
                            s, isv = divmod(t - 4, 2)
                            cm = (8 + 8 * isv) + 2 * s + m
                            dst = VC[:, m, :] if isv else XV[:, 2 * s + m, :]
                        d3, z3 = dst.rearrange("p (v t) -> p v t", v=2), CV[:, m, :].rearrange("p (v t) -> p v t", v=2)
                        dve.wait_ge(z_tap, c + 1)
                        link(stt(d3[:, :, 1:SEQ], z3[:, :, 0:SEQ - 1], col("b_conv_w", cm), d3[:, :, 1:SEQ], ALU.mult, ALU.add))
                        ins = stt(d3[:, :, 0:SEQ - 1], z3[:, :, 1:SEQ], col("b_conv_w", 6 * KT + cm), d3[:, :, 0:SEQ - 1],
                                  ALU.mult, ALU.add)
                        if t >= 4 and isv:
                            link(ins)
                            xv = XV[:, 2 * s + m, :]
                            tt(xv, xv, dst, ALU.mult).then_inc(z_conv, 1)
                        else:
                            ins.then_inc(z_conv, 1)
                    if t < 3:
                        w = FW if t < 2 else 2 * FW
                        x, n = FT[0:w, 0, :], FT[0:w, 1, :]
                        dve.wait_ge(f_mm, t + 1)
                        if t > 0:
                            dve.wait_ge(f_sin, t)
                        link(ts(x, bank[6][0:w, 0:SEQ], FBI[0:w, t:t + 1], None, ALU.add))
                        link(ts(n, x, 1.0 / TWO_PI, MAGIC, ALU.mult, ALU.add))
                        link(ts(n, n, -MAGIC, None, ALU.add))
                        link(stt(x, n, -C1, x, ALU.mult, ALU.add))
                        link(stt(x, n, -(TWO_PI - C1), x, ALU.mult, ALU.add))
                        ts(x, x, 3.1415925, -3.1415925, ALU.min, ALU.max).then_inc(f_arg, 1)
                    elif t < 7:
                        blk, hf = divmod(t - 3, 2)
                        s = slice(hf * 512, (hf + 1) * 512)
                        dve.wait_ge(f_mm, t + 1)
                        tt(HS[:, blk, s], bank[6], DC[:, blk, s], ALU.mult)
                        if blk == 0:
                            link(stt(HD[:, blk, s], bank[7], not_first, DC[:, blk, s], ALU.mult, ALU.mult))
                        else:
                            link(tt(HD[:, blk, s], bank[7], DC[:, blk, s], ALU.mult))
                        link(tt(HS[:, blk, s], HS[:, blk, s], HD[:, blk, s], ALU.add))
                        stt(HD[:, blk, s], HD[:, blk, s], -2.0, HS[:, blk, s], ALU.mult, ALU.add).then_inc(f_h, 1)

            def long_conv():
                def vt(w):
                    dve.wait_ge(c_turned, w + 1)
                    if w >= 2:
                        dve.wait_ge(c_fwd, w - 1)
                    nc.vector.tensor_copy(VX[:, w % 2, 1, :], bank[5]).then_inc(c_vt_dve, 1)

                def products(w):
                    hf, st = divmod(w, 2)
                    s = slice(hf * 512, (hf + 1) * 512)
                    dve.wait_ge(c_fwd, w + 1)
                    if w == 0:
                        dve.wait_ge(f_sev, 10)
                    if w >= 2:
                        dve.wait_ge(c_inv, w - 1)
                    tmp = [SQ[:, 0, :], SQ[:, 1, :], CV[:, 0, :], CV[:, 1, :]]
                    for b in range(2):
                        re, im, re2 = BF[:, b, s], BF[:, 2 + b, s], BF[:, 4 if b == 0 else 1, s]
                        ar, ai = bank[b], bank[2 + b]
                        tt(YS[:, w % 2, b, :], ar, re, ALU.mult).then_inc(c_prod, 1)
                        if w > 0:
                            dve.wait_ge(c_y, 4 * (w - 1) + 2 * b + 1)
                        tt(tmp[2 * b], ai, im, ALU.mult).then_inc(c_prod, 1)
                        tt(YS[:, w % 2, 2 + b, :], ar, im, ALU.mult).then_inc(c_prod, 1)
                        if w > 0:
                            dve.wait_ge(c_y, 4 * (w - 1) + 2 * b + 2)
                        tt(tmp[2 * b + 1], ai, re2, ALU.mult).then_inc(c_prod, 1)

                def skip(w):
                    hf, st = divmod(w, 2)
                    dve.wait_ge(c_inv, w + 1)
                    for c in range(4):
                        x = XV[:, 4 * hf + c, st * SEQ:(st + 1) * SEQ]
                        stt(x, x, col("b_skip", 4 * hf + c), bank[6 + c // 2][:, (c % 2) * SEQ:(c % 2 + 1) * SEQ],
                            ALU.mult, ALU.add).then_inc(c_skip, 1)

                vt(0)
                products(0)
                vt(1)
                for w in range(4):
                    if w < 3:
                        products(w + 1)
                    skip(w)
                    if w < 2:
                        vt(w + 2)

            for i in range(DEPTH):
                N = NL[i]
                pre_norm(i, 0, TOK)
                if KIND[i] == 1:
                    hyena_in()
                    long_conv()
                else:
                    attention_in(i)
                    attention(i)
                n0 = FIRST["out", i]
                for t in range(4):
                    lo(n0 + t + 2)
                    for k in mods_at(n0 + t):
                        mod(k)
                residual(i, 0, OM, N)
                pre_norm(i, 1, N)
                n0, q0 = FIRST["up", i], PAIR0["up", i]
                V = N // SEQ

                def halves(x):
                    return x[:, 0:N].rearrange("p (v t) -> p v t", v=V)

                for s in range(FM // 2):
                    lo(n0 + 2 * s + 2)
                    gate = [halves(bank[2 * ((q0 + 2 * s) % 2) + m]) for m in range(2)]
                    conv = [halves(CV[:, m, :]) for m in range(2)]
                    for m in range(2):
                        c = 2 * s + m
                        dve.wait_ge(tap0, i * FM + c + 1)
                        stt(conv[m][:, :, 1:SEQ], gate[m][:, :, 0:SEQ - 1], col("ffn_conv_w", 3 * i * FM + c),
                            conv[m][:, :, 1:SEQ], ALU.mult, ALU.add).then_inc(tap1, 1)
                    for m in range(2):
                        c = 2 * s + m
                        dve.wait_ge(tap1, i * FM + c + 1)
                        stt(conv[m][:, :, 0:SEQ - 1], gate[m][:, :, 1:SEQ], col("ffn_conv_w", (3 * i + 2) * FM + c),
                            conv[m][:, :, 0:SEQ - 1], ALU.mult, ALU.add).then_inc(conv_done, 1)
                    for k in mods_at(n0 + 2 * s):
                        mod(k)
                    lo(n0 + 2 * s + 3)
                    for m in range(2):
                        c = 2 * s + m
                        dve.wait_ge(tile_done, n0 + 2 * s + 2)
                        dve.wait_ge(silu_done, i * FM + c + 1)
                        tt(CV[:, m, 0:N], CV[:, m, 0:N], bank[2 * ((q0 + 2 * s + 1) % 2) + m][:, 0:N],
                           ALU.mult).then_inc(mf_ready, 1)
                    for k in mods_at(n0 + 2 * s + 1):
                        mod(k)
                n0 = FIRST["down", i]
                for t in range(12):
                    lo(n0 + t + 2)
                    for k in mods_at(n0 + t):
                        mod(k)
                residual(i, 1, OF, N)
                if i + 1 < DEPTH:
                    finish_mod(i + 1)
            for x in (0, 2):
                dve.wait_ge(out_turned, x + 1)
                if x:
                    dve.wait_ge(out_copied, x)
                nc.vector.tensor_copy(XR[:, x // 2, 0:512], bank[x]).then_inc(out_copied, 1)

        @block.gpsimd
        def _(pool):
            tt = nc.gpsimd.tensor_tensor
            nc.gpsimd.memset(PR[:, :, :], 0.0).then_inc(rows_clear, 1)

            def residual(i, w, O, N):
                k, seq = 2 * i + w, 4 * i + 2 * w + 1
                pool.wait_ge(rstd_ready, seq + 1)
                for c in range(1, KT, 2):
                    tt(TC[:, c, 0:N], O[:, c, 0:N], R1[:, 0:N], ALU.mult).then_inc(on_pool, 1)

            def pre_norm(i, w, N):
                seq = 4 * i + 2 * w
                pool.wait_ge(rstd_ready, seq + 1)
                for c in range(1, KT, 2):
                    tt(TC[:, c, 0:N], H[:, c, 0:N], R2[:, 0:N], ALU.mult).then_inc(hn_pool, 1)

            def attention_in(i):
                pool.wait_ge(*((tab_in, TAB_AT[i]) if i else (start_in, 32)))
                for r in range(10 if KIND[i] == 0 else 8):
                    N = NL[i] if r < 8 else TOK
                    pool.wait_ge(q_turned, turns_ahead(i) + r + 1)
                    tt(QK[:, r, 0:N], QK[:, r, 0:N], cosT[:, 0:N], ALU.mult).then_inc(q_cos, 1)

            def long_conv():
                pool.wait_ge(f_h, 4)
                pool.dma_start(IF[:, :, :], a["k_idft"].rearrange("(j p) t -> p j t", p=P)).then_inc(tab_in, 16)

                def y(w):
                    tmp = [SQ[:, 0, :], SQ[:, 1, :], CV[:, 0, :], CV[:, 1, :]]
                    for b in range(2):
                        pool.wait_ge(c_prod, 8 * w + 4 * b + 2)
                        y = YS[:, w % 2, b, :]
                        tt(y, y, tmp[2 * b], ALU.subtract).then_inc(c_y, 1)
                        pool.wait_ge(c_prod, 8 * w + 4 * b + 4)
                        y = YS[:, w % 2, 2 + b, :]
                        tt(y, y, tmp[2 * b + 1], ALU.add).then_inc(c_y, 1)

                def gate(w):
                    hf, st = divmod(w, 2)
                    s = slice(st * SEQ, (st + 1) * SEQ)
                    for c in range(4):
                        pool.wait_ge(c_skip, 4 * w + c + 1)
                        tt(XV[:, 4 * hf + c, s], XV[:, 4 * hf + c, s], X0[:, 4 * hf + c, s], ALU.mult).then_inc(c_gated, 1)
                    for c in range(4):
                        pool.wait_ge(c_hi, 4 * w + c + 1)
                        tt(UL[:, 4 * hf + c, s], XV[:, 4 * hf + c, s], UH[:, 4 * hf + c, s].bitcast(F32),
                           ALU.subtract).then_inc(c_lo, 1)

                y(0)
                for w in range(4):
                    if w < 3:
                        y(w + 1)
                    gate(w)

            def load_tables(i):
                pool.wait_ge(tile_done, FIRST["in", i])
                if KIND[i] == 0:
                    pool.dma_start(RC[:, 0:2 * TOK + P], a["k_rope_a"]).then_inc(tab_in, 16)
                elif KIND[i] == 2:
                    pool.dma_start(RC[:, :], a["k_rope_c"]).then_inc(tab_in, 16)

            def load_filter():
                pool.wait_ge(u_ready, 2 * KT + KT)
                for dst, src in ((FA[0:FEMB, 0, :], a["k_zt"]), (FWT[0:FEMB, 0:FW], a["b_f_w1"][0]),
                                 (FWT[0:FW, FW:2 * FW], a["b_f_w2"][0]), (FWT[0:FW, 2 * FW:3 * FW], a["b_f_w3"][0]),
                                 (FWT[0:FW, 3 * FW:4 * FW], a["b_f_w3"][0]),
                                 (FBI[0:FW, 0:1], a["b_f_b1"].rearrange("o f -> f o")),
                                 (FBI[0:FW, 1:2], a["b_f_b2"].rearrange("o f -> f o")),
                                 (FBI[0:FW, 2:3], a["b_f_b3"].rearrange("o f -> f o")),
                                 (FBI[FW:2 * FW, 2:3], a["b_f_b3"].rearrange("o f -> f o")),
                                 (W4[0:FW, :], a["b_f_w4"][0, :, 0:D]), (W4[FW:2 * FW, :], a["b_f_w4"][0, :, D:2 * D]),
                                 (DC[:, :, :], a["k_decay"].rearrange("(b p) d -> p b d", p=P)),
                                 (DF[:, :, :], a["k_dft"].rearrange("(b p) d -> p b d", p=P))):
                    pool.dma_start(dst, src).then_inc(tab_in, 16)

            for i in range(DEPTH):
                N = NL[i]
                if i > 0:
                    load_tables(i)
                pre_norm(i, 0, TOK)
                if KIND[i] == 1:
                    load_filter()
                    long_conv()
                else:
                    attention_in(i)
                residual(i, 0, OM, N)
                pre_norm(i, 1, N)
                for c in range(FM):
                    pool.wait_ge(mh_ready, i * FM + c + 1)
                    tt(ML[:, c, 0:N], CV[:, c % 2, 0:N], MH[:, c, 0:N].bitcast(F32), ALU.subtract).then_inc(ml_ready, 1)
                residual(i, 1, OF, N)


SLAB_AT = 8320
ROPE_COLS = 2 * TOK + 5 * P + 2 * TOK
N_ROW_DMAS = sum((ROW0[name] + k - 1) // P - ROW0[name] // P + 1 for name, k in ROWS)
TAB_AT = {1: 16 * 13, 2: 16 * 15, 3: 16 * 16}


def QCOS(i):
    return sum(10 if KIND[j] == 0 else 8 for j in range(i) if KIND[j] != 1)


def MASKED(i):
    return sum(C_HEADS for j in range(i) if KIND[j] == 2)


def CTXG(i):
    return sum({0: A_HEADS, 1: 0, 2: C_HEADS}[KIND[j]] for j in range(i))


_INS = ["x", "c", "ctx", "c_ctx", "mod_w", "mod_b", "norm_g", "ffn_w_up", "ffn_conv_w", "ffn_conv_b", "ffn_w_down",
        "a_w_qkv", "a_q_gain", "a_k_gain", "a_w_out", "b_w_in", "b_b_in", "b_conv_w", "b_conv_b", "b_f_w1", "b_f_b1",
        "b_f_w2", "b_f_b2", "b_f_w3", "b_f_b3", "b_f_w4", "b_skip", "b_w_out", "b_b_out", "c_w_qkv", "c_b_qkv",
        "c_sink", "c_w_out", "c_b_out"]


def kernel(**inputs):
    import concourse.bacc as bacc
    from concourse.bass_utils import run_bass_kernel_spmd

    nc = bacc.Bacc("TRN2", target_bir_lowering=False, num_devices=1,
                   dynamic_dma_scratch_size=8192)
    arrays = {name: np.ascontiguousarray(inputs[name]) for name in _INS}
    arrays.update(constants())
    aps = {name: nc.dram_tensor("in_" + name, v.shape, mybir.dt.from_np(v.dtype), kind="ExternalInput").ap()
           for name, v in arrays.items()}
    out = nc.dram_tensor("out_0", (1, SEQ, D), F32, kind="ExternalOutput").ap()
    build(nc, aps, out)
    r = run_bass_kernel_spmd(nc, [{"in_" + name: v for name, v in arrays.items()}], core_ids=[0])
    return r.results[0]["out_0"]
```

```python
import math
from contextlib import ExitStack

import numpy as np

import concourse.bass as bass
from concourse import mybir

F32 = mybir.dt.float32
F32R = mybir.dt.float32r
ALU = mybir.AluOpType
ACT = mybir.ActivationFunctionType
AX = mybir.AxisListType

P = 128
D = 1024
KT = D // P
SEQ = 256
CTX = 256
TOK = SEQ + CTX
DEPTH = 4
GRID_W = 64
DFF = 2816
FM = DFF // P
EPS = 1e-6
TW = 256
A_HEADS, A_KV, A_DH = 8, 2, 128
C_HEADS, C_KV, C_DH = 16, 2, 64
FEMB, FW = 33, 64
NMOD = 6
MB = NMOD * D // TW
NFREQ = 2 * SEQ
KIND = [i % 3 for i in range(DEPTH)]

ROWS = [("norm_g", DEPTH * 4 * KT), ("ffn_conv_w", DEPTH * 3 * FM), ("ffn_conv_b", DEPTH * FM),
        ("mod_b", DEPTH * NMOD * KT), ("c", KT), ("c_ctx", KT), ("a_q_gain", 2), ("a_k_gain", 2),
        ("b_b_in", 3 * KT), ("b_conv_w", 9 * KT), ("b_conv_b", 3 * KT), ("b_skip", KT), ("b_b_out", KT),
        ("c_b_qkv", 10), ("c_b_out", KT)]
ROW0 = {}
_n = 0
for _name, _k in ROWS:
    ROW0[_name] = _n
    _n += _k
NPAR = -(-_n // P)

TILES = []
FIRST = {}
for _i in range(DEPTH):
    _k, _j = KIND[_i], _i // 3
    FIRST["in", _i] = len(TILES)
    if _k == 0:
        TILES += [("a_w_qkv", _j, 0, KT, TW * t, TW) for t in range(6)]
    elif _k == 1:
        TILES += [("b_w_in", _j, 0, KT, TW * t, TW) for t in range(4)]
        for _t in range(4):
            TILES += [("b_w_in", _j, 0, KT, D + TW * _t, TW), ("b_w_in", _j, 0, KT, 2 * D + TW * _t, TW)]
    else:
        TILES += [("c_w_qkv", _j, 0, KT, TW * t, TW) for t in range(4)]
        TILES += [("c_w_qkv", _j, 0, KT, D, P), ("c_w_qkv", _j, 0, KT, D + P, P)]
    FIRST["out", _i] = len(TILES)
    TILES += [("abc"[_k] + "_w_out", _j, 0, KT, TW * t, TW) for t in range(4)]
    FIRST["up", _i] = len(TILES)
    for _t in range(FM // 2):
        TILES += [("ffn_w_up", _i, 0, KT, TW * _t, TW), ("ffn_w_up", _i, 0, KT, DFF + TW * _t, TW)]
    FIRST["down", _i] = len(TILES)
    for _t in range(4):
        TILES += [("ffn_w_down", _i, r, min(8, FM - r), TW * _t, TW) for r in range(0, FM, 8)]
NT = len(TILES)


def constants():
    f = np.float32
    out = {}

    def rope(dh):
        axis = dh // 2
        inv = np.power(f(10000.0), -np.arange(0, axis, 2, dtype=f) / f(axis)).astype(f)
        t = np.arange(SEQ)
        ang = np.concatenate([(t // GRID_W).astype(f)[:, None] * inv[None],
                              (t % GRID_W).astype(f)[:, None] * inv[None]], axis=-1)
        half = dh // 2
        cos, sin = np.ones((P, TOK), f), np.zeros((P, TOK), f)
        for p in range(P):
            cos[p, :SEQ] = np.cos(ang[:, p % half]).astype(f)
            sin[p, :SEQ] = np.sin(ang[:, p % half]).astype(f)
        rot = np.zeros((P, P), f)
        for p in range(P):
            if p % dh < half:
                rot[p + half, p] = -1.0
            else:
                rot[p - half, p] = 1.0
        return cos, sin, rot

    cos, sin, rot = rope(A_DH)
    out["k_rope_a"] = np.concatenate([cos, sin, rot], axis=1)
    cos, sin, rot = rope(C_DH)
    mats = [rot]
    for kv in range(C_KV):
        dup = np.zeros((P, P), f)
        for p in range(P):
            dup[C_DH * kv + p % C_DH, p] = 1.0
        mats += [dup, (rot.astype(np.float64) @ dup).astype(f)]
    mask = np.zeros((2, P, TOK), f)
    for b in range(2):
        q = b * P + np.arange(P)[:, None]
        mask[b, :, :SEQ] = np.where(np.abs(np.arange(SEQ)[None, :] - q) <= 128, 0.0, -1e30)
    out["k_rope_c"] = np.concatenate([cos, sin] + mats + [mask[0], mask[1]], axis=1)
    out["k_ident"] = np.concatenate([np.eye(P, dtype=f), 1.0 - np.eye(P, 1, dtype=f)], axis=1)

    t = np.linspace(0.0, 1.0, SEQ, dtype=f)[:, None]
    omega = (f(2.0 * math.pi / SEQ) * np.arange(SEQ, dtype=f)).astype(f)
    bands = np.linspace(1e-4, 15, 16, dtype=f)
    ang = (omega[:, None] * bands[None, :]).astype(f)
    z = np.concatenate([t, np.cos(ang), -np.sin(ang)], axis=-1).astype(f)
    out["k_zt"] = np.ascontiguousarray(z.T)
    rates = np.abs(np.linspace(math.log(1e-2) / 0.3, math.log(1e-2) / 1.5, D, dtype=f))
    out["k_decay"] = np.exp(-t * rates[None, :]).astype(f)

    s = np.arange(SEQ, dtype=np.float64)[:, None]
    fr = np.arange(SEQ, dtype=np.float64)[None, :]
    th = 2 * np.pi * ((s * fr) % NFREQ) / NFREQ
    re, im = np.cos(th), -np.sin(th)
    nyq = np.cos(np.pi * s)
    imn = np.concatenate([nyq, im[:, 1:]], axis=1)
    ren = np.concatenate([nyq, re[:, 1:P]], axis=1)
    out["k_dft"] = np.concatenate([re, imn, ren, im[:, :P]], axis=1).astype(f)
    w = np.full((SEQ, 1), 2.0 / NFREQ)
    w[0] = 1.0 / NFREQ
    inv_re = w * np.cos(th.T)
    inv_im = -2.0 / NFREQ * np.sin(th.T)
    inv_im[0] = 1.0 / NFREQ * np.cos(np.pi * np.arange(SEQ))
    out["k_idft"] = np.concatenate([inv_re, inv_im], axis=0).astype(f)
    return out


def build(nc, a, out):
    es = ExitStack()
    with es:
        def sem(name):
            return es.enter_context(nc.semaphore(name))

        slab_words = 54400
        es.enter_context(nc.sbuf_tensor("slab", [P, slab_words + 8], F32))
        base = SLAB_AT
        cur = [base]

        def place(name, shape, dt=F32, at=None):
            n = -(-4 * math.prod(shape[1:]) // 32) * 32
            off = cur[0] if at is None else at
            if at is None:
                cur[0] += n
                assert cur[0] <= base + 4 * slab_words, (name, cur[0] - base, 4 * slab_words)
            return nc.alloc_sbuf_tensor_at(name, shape, dt, offset=off)

        H = place("h", [P, KT, TOK])
        U_AT = cur[0]
        UH = place("u_hi", [P, KT, TOK], F32R)
        UL = place("u_lo", [P, KT, TOK], F32R)
        M0 = cur[0]
        MH = place("mid_hi", [P, FM, TOK], F32R)
        ML = place("mid_lo", [P, FM, TOK], F32R)
        M_END = cur[0]
        RAW = place("w_raw", [P, 2, KT * TW])
        WH = place("w_hi", [P, 2, KT * TW], F32R)
        WL = place("w_lo", [P, 2, KT * TW], F32R)
        SQ_AT = cur[0]
        SQ = place("squares", [P, 2, TOK])
        CV = place("conv", [P, 2, TOK])
        MR = place("mod_raw", [P, 2, 4, TW])
        MA_AT = cur[0]
        MA = place("mod_acc", [P, 2, 2, TW])
        par = place("par", [P, NPAR * P])
        ident_t = place("ident", [P, P + 1])
        ones = place("ones", [P, P])
        S2 = place("silu_c", [P, 2, KT])
        SQA = place("square_sum", [P, TOK])
        modv = place("modv", [P, 2, NMOD * KT])
        coef = place("coef", [P, 2, 4, KT])
        small = place("small", [P, 2, 5, 4])
        q_scale = place("q_scale", [P, 2, 4 * A_HEADS])
        sinkb = place("sink", [P, C_HEADS])
        eps = place("eps", [P, 1])
        ident = ident_t[:, 0:P]
        not_first = ident_t[:, P:P + 1]
        OF = place("o_mlp", [P, KT, TOK], at=U_AT)
        RMS_O, RMS_H = CV[:, 0, :], CV[:, 1, :]

        def region(*items):
            got, at = [], M0
            for name, shape, off in items:
                at = M0 + off if off is not None else at
                n = 4 * math.prod(shape[1:])
                assert at + n <= M_END, name
                got.append(place(name, shape, at=at))
                at += n
            return got

        OM, TC = region(("o_mixer", [P, KT, TOK], 0), ("normed", [P, KT, TOK], None))
        (QK, KD, VT, RT, RC, SM, PB, PT, XR, PR) = region(
            ("qkv", [P, 12, TOK], 0), ("k_dup", [P, C_KV, TOK], None), ("v_tok", [P, 4, 2 * P], None),
            ("rope_tmp", [P, 2, TOK], None), ("rope_tab", [P, ROPE_COLS], None), ("scores", [P, 2, TOK], None),
            ("probs", [P, 2, 3, TOK], None), ("probs_t", [P, 2, 3, TOK], None),
            ("x_rows", [P, 4, D], 4 * (26 * TOK + ROPE_COLS)), ("par_rows", [P, NPAR, P], None))
        (X0, XV, BF, DF, HS, HD, DC, W4, FWT, FBI) = region(
            ("x0", [P, KT, TOK], 0), ("x1v", [P, KT, TOK], None), ("filter_spec", [P, 5, D], None),
            ("dft", [P, 2, 6 * P], None), ("h_sum", [P, 2, D], None), ("h_diff", [P, 2, D], None),
            ("decay", [P, 2, D], None), ("f_w4", [P, D], None), ("f_w", [P, 4 * FW], None), ("f_b", [P, 3], None))
        YS, VX, IF = region(("y_spec", [P, 2, 4, 512], 4 * (16 * TOK + 5 * D + 12 * P)),
                            ("x1v_tok", [P, 2, 2, 512], None), ("idft", [P, 4, SEQ], None))
        MG = [place("mod_group0", [P, KT, 512], at=U_AT), place("mod_group1", [P, KT, 512], at=U_AT + 16 * D)]
        MG += region(("mod_group2", [P, KT, 512], 0), ("mod_group3", [P, KT, 512], None))
        (MROW,) = region(("mod_rows", [P, MOD0 // 4 * 512], 4 * (18 * TOK + ROPE_COLS)))
        FA = place("f_act", [P, 2, SEQ], at=SQ_AT)
        FT = place("f_arg", [P, 2, SEQ], at=SQ_AT + 8 * SEQ)
        VC = place("v_conv", [P, 2, TOK], at=MA_AT)
        cosT, sinT = RC[:, 0:TOK], RC[:, TOK:2 * TOK]

        def rope_mat(m):
            return RC[:, 2 * TOK + m * P:2 * TOK + (m + 1) * P]
        maskT = RC[:, 2 * TOK + 5 * P:ROPE_COLS].rearrange("p (b k) -> p b k", b=2)

        lo4 = es.enter_context(nc.psum_tensor("lo4", [P, 4, 512], F32))
        stat = es.enter_context(nc.psum_tensor("stat", [P, 512], F32))
        modp = es.enter_context(nc.psum_tensor("modp", [P, 512], F32))
        hi2 = es.enter_context(nc.psum_tensor("hi2", [P, 2, 512], F32))
        bank = [lo4[:, 0, :], lo4[:, 1, :], lo4[:, 2, :], lo4[:, 3, :], stat[:, :], modp[:, :], hi2[:, 0, :], hi2[:, 1, :]]

        raw_in = [sem("raw_in0"), sem("raw_in1")]
        hi_ready, lo_ready, tile_done = sem("hi_ready"), sem("lo_ready"), sem("tile_done")
        mod_in = [sem("mod_in0"), sem("mod_in1")]
        mod_step, mod_reduced, mod_final = sem("mod_step"), sem("mod_reduced"), sem("mod_final")
        rows_in, rows_clear, const_in, x_in, tab_in = (sem("rows_in"), sem("rows_clear"), sem("const_in"),
                                                       sem("x_in"), sem("tab_in"))
        start_in = sem("start_in")
        consts_set, par_turned, par_ready, silu_ready = (sem("consts_set"), sem("par_turned"), sem("par_ready"),
                                                         sem("silu_ready"))
        x_turned, h_loaded = sem("x_turned"), sem("h_loaded")
        sq_ready, sq_added, stat_step, root_ready = (sem("sq_ready"), sem("sq_added"), sem("stat_step"),
                                                     sem("root_ready"))
        gated, h_even, h_odd = sem("gated"), sem("h_even"), sem("h_odd")
        un_ready, uh_ready, us_ready = sem("un_ready"), sem("uh_ready"), sem("us_ready")
        u_even, u_odd = sem("u_even"), sem("u_odd")
        group_in = [sem(f"group_in{g}") for g in range(4)]
        group_done, group_rows, group_cols = sem("group_done"), sem("group_rows"), sem("group_cols")
        o_ready = sem("o_ready")
        tap0, tap1, conv_done, silu_done = sem("tap0"), sem("tap1"), sem("conv_done"), sem("silu_done")
        mf_ready, mh_ready, ml_ready = sem("mf_ready"), sem("mh_ready"), sem("ml_ready")
        out_turned, out_copied, out_stored = sem("out_turned"), sem("out_copied"), sem("out_stored")
        q_evac, q_sq, q_turned, q_root, q_cos, q_roped = (sem("q_evac"), sem("q_sq"), sem("q_turned"), sem("q_root"),
                                                          sem("q_cos"), sem("q_roped"))
        v_turned, v_ready = sem("v_turned"), sem("v_ready")
        s_ready, s_masked, s_max, s_exp, s_norm = (sem("s_ready"), sem("s_masked"), sem("s_max"), sem("s_exp"),
                                                   sem("s_norm"))
        p_turned, p_ev_lat, p_ev_ctx, pv_done, ao_hi, ao_lo = (sem("p_turned"), sem("p_ev_lat"), sem("p_ev_ctx"),
                                                               sem("pv_done"), sem("ao_hi"), sem("ao_lo"))
        z_evac, z_tap, z_conv = sem("z_evac"), sem("z_tap"), sem("z_conv")
        f_mm, f_arg, f_sin, f_h, f_spec, f_sev = (sem("f_mm"), sem("f_arg"), sem("f_sin"), sem("f_h"), sem("f_spec"),
                                                  sem("f_sev"))
        c_turned, c_vt_act, c_vt_dve, c_fwd, c_prod, c_y = (sem("c_turned"), sem("c_vt_act"), sem("c_vt_dve"),
                                                            sem("c_fwd"), sem("c_prod"), sem("c_y"))
        c_inv, c_skip, c_gated, c_hi, c_lo = sem("c_inv"), sem("c_skip"), sem("c_gated"), sem("c_hi"), sem("c_lo")
        dve_chain = sem("dve_chain")

        NL = [TOK if i < DEPTH - 1 else SEQ for i in range(DEPTH)]

        def col(name, r, n=1):
            return par[:, ROW0[name] + r:ROW0[name] + r + n]

        ATT = [i for i in range(DEPTH) if KIND[i] != 1]
        EV = {i: 12 if KIND[i] == 0 else 10 for i in ATT}
        HEADS = {i: A_HEADS if KIND[i] == 0 else C_HEADS for i in ATT}
        VCH = {i: 2 if KIND[i] == 0 else 1 for i in ATT}

        def ahead(per, i):
            return sum(per[j] for j in ATT if j < i)

        def turns_ahead(i):
            return 10 * len([j for j in ATT if j < i])

        def norms_ahead(i):
            return 3 * len([j for j in ATT if j < i and KIND[j] == 0])

        PAIRS = []
        for i in range(DEPTH):
            PAIRS += [("in", i, t) for t in range(12 if KIND[i] == 1 else 6)]
            PAIRS += [("out", i, t) for t in range(4)]
            PAIRS += [("up", i, t) for t in range(FM)]
            PAIRS += [("down", i, t) for t in range(4)]
        PAIR0 = {(ph, i): q for q, (ph, i, t) in enumerate(PAIRS) if t == 0}

        def released(q):
            ph, i, t = PAIRS[q]
            if ph == "in" and KIND[i] == 0:
                return q_evac, ahead(EV, i) + 2 * t + 2
            if ph == "in" and KIND[i] == 2:
                return q_evac, ahead(EV, i) + (2 * t + 2 if t < 4 else t + 5)
            if ph == "in":
                return z_evac, 2 * t + 2
            if ph == "out":
                return o_ready, 2 * i * KT + 2 * t + 2
            if ph == "down":
                return o_ready, (2 * i + 1) * KT + 2 * t + 2
            return (conv_done, i * FM + t + 2) if t % 2 == 0 else (mf_ready, i * FM + t + 1)

        def v_bank(i, j):
            return bank[2 * ((PAIR0["in", i] + 4 + j) % 2)]

        def turned_bank(i, r):
            return bank[2 * ((PAIR0["in", i] + 4) % 2) + 1 if KIND[i] == 0 and r == 9 else 6 + r % 2]

        OV = [NL[k // 2] // SEQ for k in range(2 * DEPTH)]
        UV = [2 if k % 2 == 0 else OV[k] for k in range(2 * DEPTH)]
        U0 = [KT * sum(UV[:k]) for k in range(2 * DEPTH)]
        R0 = [KT * sum(OV[:k]) for k in range(2 * DEPTH)]
        SQO, SQH, ROOT = {}, {}, {}
        SUMMED = {}
        USED = []
        nr = na = nm = 0
        for k in range(2 * DEPTH):
            SQH[k] = len(USED)
            for v in range(UV[k]):
                USED += [(stat_step, nm + c + 1) for c in range(KT)]
                nm += KT
                SUMMED["h", k, v] = nm
                ROOT["h", k, v], nr = nr, nr + 1
            SQO[k] = len(USED)
            USED += [(sq_added, na + max(1, c)) for c in range(KT - 2)] + [(stat_step, nm + 2), (stat_step, nm + 3)]
            na, nm = na + KT - 3, nm + 3
            SUMMED["o", k] = nm
            ROOT["o", k], nr = nr, nr + 1

        def u_part(k, v, c):
            return u_odd if c % 2 else u_even, (U0[k] + KT * v) // 2 + c // 2 + 1

        MODS, HEAD_MODS = {}, {}
        k = MOD0
        for t in range(5):
            w = 2 if t < 2 else 1
            MODS[t] = list(range(k, k + w))
            k += w
        for h in range(A_HEADS):
            w = 2 if h < 3 else 1
            HEAD_MODS[h] = list(range(k, k + w))
            k += w
        for i in range(DEPTH - 1):
            for t in range(3):
                MODS[FIRST["out", i] + t] = [k, k + 1]
                k += 2
            for t in range(FM):
                w = 2 if i == 0 and t % 2 == 1 and t < 12 else 1
                MODS[FIRST["up", i] + t] = list(range(k, k + w))
                k += w
            for t in range(10):
                MODS[FIRST["down", i] + t] = [k, k + 1]
                k += 2
            assert k == 2 * MB * (i + 2), k

        def mods_at(n):
            return MODS.get(n, [])

        MID, END, AFTER_IN = {}, {}, []
        for n, ks in MODS.items():
            for x in ks:
                late = x == ks[-1]
                if n < 6 and n + 1 + late > 5:
                    AFTER_IN.append(x)
                elif late and n != FIRST["out", 0] + 2:
                    MID.setdefault(n + 2, []).append(x)
                else:
                    END.setdefault(n + 1, []).append(x)

        block = es.enter_context(nc.Block())

        @block.sync
        def _(sp):
            sp.wait_ge(rows_clear, 1)
            for name, k in ROWS:
                src = a[name]
                flat = src.rearrange({1: "(r q) -> r q", 2: "a (r q) -> (a r) q",
                                      3: "a b (r q) -> (a b r) q"}[len(src.shape)], q=P)
                r = 0
                while r < k:
                    g = ROW0[name] + r
                    m = min(k - r, P - g % P)
                    sp.dma_start(PR[g % P:g % P + m, g // P, :], flat[r:r + m, :]).then_inc(rows_in, 16)
                    r += m
            sp.dma_start(ident_t[:, :], a["k_ident"]).then_inc(const_in, 16)

            def raw(n):
                if n >= NT:
                    return
                name, j, r0, nr, c0, w = TILES[n]
                if n >= 2:
                    sp.wait_ge(lo_ready, n - 1)
                src = a[name][j, r0 * P:(r0 + nr) * P, c0:c0 + w].rearrange("(k p) n -> p k n", p=P)
                sp.dma_start(RAW[:, n % 2, 0:nr * w].rearrange("p (k n) -> p k n", n=w),
                             src).then_inc(raw_in[n % 2], 16)

            def mod(k):
                layer, r = divmod(k, 2 * MB)
                if k >= MOD0 + 2:
                    sp.wait_ge(mod_step, 8 * (k - MOD0 - 1))
                src = a["mod_w"][layer, (r % 2) * 4 * P:(r % 2) * 4 * P + 4 * P, (r // 2) * TW:(r // 2) * TW + TW]
                sp.dma_start(MR[:, k % 2, :, :], src.rearrange("(k p) n -> p k n", p=P)).then_inc(mod_in[k % 2], 16)

            def group(g):
                if g >= 4:
                    sp.wait_ge(group_done, g - 3)
                sp.dma_start(MG[g % 4][:, :, :], a["mod_w"][0, :, g * 512:(g + 1) * 512].rearrange(
                    "(k p) n -> p k n", p=P)).then_inc(group_in[g % 4], 16)

            group(0)
            group(1)
            for t in range(4):
                src = a["x"] if t < 2 else a["ctx"]
                sp.dma_start(XR[:, t, :], src[0, (t % 2) * P:(t % 2) * P + P, :]).then_inc(x_in, 16)
            group(2)
            group(3)
            raw(0)
            raw(1)
            for g in range(4, MOD0 // 4):
                group(g)
            mod(MOD0)
            mod(MOD0 + 1)
            sp.dma_start(RC[:, 0:2 * TOK + P], a["k_rope_a"]).then_inc(start_in, 16)
            sp.dma_start(sinkb[:, :], a["c_sink"].broadcast_to([P, C_HEADS])).then_inc(start_in, 16)
            raw(2)
            raw(3)
            for n in range(NT):
                if n == FIRST["out", 0]:
                    for h in range(A_HEADS):
                        for x in HEAD_MODS[h]:
                            mod(x + 2)
                raw(n + 4)
                for x in mods_at(n):
                    if x + 2 < 2 * MB * DEPTH:
                        mod(x + 2)

            for t in range(2):
                sp.wait_ge(out_copied, 2 * t + 2)
                sp.dma_start(out[0, t * P:t * P + P, :], XR[:, t, :]).then_inc(out_stored, 16)
            sp.wait_ge(out_stored, 32)

        @block.tensor
        def _(pe):
            mm = nc.tensor.matmul

            def reduce_mod(k):
                layer, r = divmod(k, 2 * MB)
                if r % 2 == 0:
                    return
                if r == 1 and layer > 0:
                    pe.wait_ge(mod_final, layer + 1)
                pe.wait_ge(mod_step, 8 * (k - MOD0 + 1))
                for v in range(2):
                    for cc in range(2):
                        at = v * NMOD * KT + (r // 2) * 2 + cc
                        last = mm(modp[:, at:at + 1], MA[:, k // 2 % 2, v, cc * P:(cc + 1) * P], ones[:, 0:1],
                                  start=True, stop=True)
                last.then_inc(mod_reduced, 1)

            def tile(n, q, N, hi, lo, first, last, kt0=0, arrive=None, s0=0, done=True):
                nr, w = TILES[n][3], TILES[n][5]
                b0 = 2 * (q % 2)
                if first and q >= 2:
                    pe.wait_ge(*released(q - 2))
                pe.wait_ge(lo_ready, n + 1)
                h3 = WH[:, n % 2, 0:nr * w].rearrange("p (k n) -> p k n", n=w)
                l3 = WL[:, n % 2, 0:nr * w].rearrange("p (k n) -> p k n", n=w)
                for k in range(nr):
                    if arrive:
                        arrive(kt0 + k)
                    for m in range(w // P):
                        o = bank[b0 + m][:, s0:N]
                        c = slice(m * P, (m + 1) * P)
                        x, y = hi[:, kt0 + k, s0:N], lo[:, kt0 + k, s0:N]
                        mm(o, h3[:, k, c], x, start=(first and k == 0), stop=False)
                        mm(o, h3[:, k, c], y, start=False, stop=False)
                        ins = mm(o, l3[:, k, c], x, start=False, stop=(last and k == nr - 1))
                    if done and k == nr // 2 - 1:
                        for x in MID.get(n, []):
                            reduce_mod(x)
                if done:
                    ins.then_inc(tile_done, 1)
                    for x in END.get(n, []):
                        reduce_mod(x)

            def first_tiles(n, q, sub, widths):
                V = UV[sub]
                for v in range(V):
                    for t in range(2):
                        if v * SEQ < widths[t]:
                            tile(n + t, q + t, (v + 1) * SEQ, UH, UL, True, True, s0=v * SEQ,
                                 arrive=(lambda k, v=v: pe.wait_ge(*u_part(sub, v, k))) if t == 0 else None,
                                 done=(v + 1) * SEQ >= widths[t])

            def sum_squares(s, out, first, last):
                pe.wait_ge(sq_ready, s + 1)
                mm(out, ones[:, :], SQ[:, s % 2, 0:out.shape[1]], start=first, stop=last).then_inc(stat_step, 1)

            def o_norm(k):
                if k > 0:
                    pe.wait_ge(root_ready, ROOT["o", k])
                out = bank[4][:, 0:NL[k // 2]]
                pe.wait_ge(sq_added, (k + 1) * (KT - 3))
                mm(out, ones[:, :], SQA[:, 0:NL[k // 2]], start=True, stop=False).then_inc(stat_step, 1)
                for c in (KT - 2, KT - 1):
                    sum_squares(SQO[k] + c, out, False, c == KT - 1)

            def u_norm(k):
                for v in range(UV[k]):
                    for c in range(KT):
                        sum_squares(SQH[k] + KT * v + c, bank[6 + v][:, 0:SEQ], c == 0, c == KT - 1)

            pe.wait_ge(const_in, 16)
            pe.wait_ge(rows_in, 16 * N_ROW_DMAS)
            for t in range(NPAR):
                last = nc.tensor.transpose(bank[6 + t // 4][:, (t % 4) * P:(t % 4 + 1) * P], PR[:, t, :], ident)
            last.then_inc(par_turned, 1)
            pe.wait_ge(x_in, 64)
            for c in range(KT):
                if c >= 4:
                    pe.wait_ge(h_loaded, c - 3)
                for t in range(4):
                    last = nc.tensor.transpose(bank[c % 4][:, t * P:(t + 1) * P], XR[:, t, c * P:(c + 1) * P], ident)
                last.then_inc(x_turned, 1)
            pe.wait_ge(consts_set, 1)
            pe.wait_ge(silu_ready, 1)
            for g in range(MOD0 // 4):
                pe.wait_ge(group_in[g % 4], 16 * (g // 4 + 1))
                pe.wait_ge(h_loaded, KT)
                if g >= 4:
                    pe.wait_ge(group_rows, g - 3)
                for k in range(KT):
                    last = mm(bank[g % 4][0:2, :], S2[:, :, k], MG[g % 4][:, k, :], start=(k == 0), stop=(k == KT - 1))
                last.then_inc(group_done, 1)
            pe.wait_ge(group_rows, MOD0 // 4)
            for c in range(2 * MOD0 // 2):
                last = mm(modp[:, c:c + NMOD * KT + 1:NMOD * KT], MROW[0:2, c * P:(c + 1) * P], ident[0:2, 0:2],
                          start=True, stop=True)
            last.then_inc(group_cols, 1)

            def turn_q(i, r):
                g = turns_ahead(i) + r
                N = NL[i] if r < 8 else TOK
                if r >= 2:
                    pe.wait_ge(q_roped, g - 1)
                if r == 0 and i > 0:
                    pe.wait_ge(mod_final, i + 2)
                if KIND[i] == 0 and (r == 8 or r == 9 and i == 0):
                    pe.wait_ge(q_root, norms_ahead(i) + r - 7)
                if r == 0:
                    pe.wait_ge(*((tab_in, TAB_AT[i]) if i else (start_in, 32)))
                if KIND[i] == 0:
                    pe.wait_ge(q_evac, ahead(EV, i) + r + 1)
                    if r < 8:
                        for b in range(N // P):
                            mm(bank[4][:, 4 * r + b:4 * r + b + 1], SQ[:, r % 2, b * P:(b + 1) * P], ones[:, 0:1],
                               start=True, stop=True)
                    else:
                        mm(bank[QSUM(i, r)][:, 0:N], ones[:, :], SQ[:, r % 2, 0:N], start=True, stop=True)
                    mm(turned_bank(i, r)[:, 0:N], rope_mat(0), QK[:, r, 0:N], start=True, stop=True).then_inc(q_turned, 1)
                elif r < 8:
                    pe.wait_ge(q_evac, ahead(EV, i) + r + 1)
                    mm(bank[6 + r % 2][:, 0:N], rope_mat(0), QK[:, r, 0:N], start=True, stop=True).then_inc(q_turned, 1)
                else:
                    pe.wait_ge(q_evac, ahead(EV, i) + 9)
                    mm(bank[4 + r % 2], rope_mat(1 + 2 * (r - 8)), QK[:, 8, :], start=True, stop=True)
                    mm(bank[6 + r % 2], rope_mat(2 + 2 * (r - 8)), QK[:, 8, :], start=True, stop=True).then_inc(q_turned, 1)

            def turn_v(i, j):
                pe.wait_ge(q_evac, ahead(EV, i) + EV[i])
                src = QK[:, EV[i] - VCH[i] + j, :]
                for t in range(4):
                    last = nc.tensor.transpose(v_bank(i, j)[:, t * P:(t + 1) * P], src[:, t * P:(t + 1) * P], ident)
                last.then_inc(v_turned, 1)

            def attention(i):
                G, A = ahead(HEADS, i), KIND[i] == 0
                ctx = NL[i] == TOK
                part = A_HEADS // A_KV if A else C_HEADS // C_KV

                def scores(h):
                    g = G + h
                    if h == 0:
                        pe.wait_ge(q_roped, turns_ahead(i) + (9 if A else 10))
                        if A:
                            pe.wait_ge(q_root, norms_ahead(i) + 3)
                    else:
                        pe.wait_ge(*((s_exp, g) if A else (s_masked, MASKED(i) + h)))
                    if A and h == part:
                        pe.wait_ge(q_roped, turns_ahead(i) + 10)
                    if A:
                        q, k = QK[:, h, :], QK[:, 8 + h // part, :]
                    else:
                        ps = slice(64 * (h % 2), 64 * (h % 2) + 64)
                        q, k = QK[ps, h // 2, :], KD[ps, h // part, :]
                    for b in range(2):
                        last = mm(bank[6 + b], q[:, b * P:(b + 1) * P], k[:, 0:TOK], start=True, stop=True)
                    if ctx:
                        if h > 0:
                            pe.wait_ge(s_exp, g)
                        for b in range(2):
                            last = mm(bank[4][:, b * CTX:(b + 1) * CTX], q[:, SEQ + b * P:SEQ + (b + 1) * P],
                                      k[:, SEQ:TOK], start=True, stop=True)
                    last.then_inc(s_ready, 1)

                def turn(h):
                    g = G + h
                    pe.wait_ge(s_norm, g + 1)
                    if h == 0:
                        pe.wait_ge(v_ready, ahead(VCH, i) + VCH[i])
                        pe.wait_ge(*released(PAIR0["out", i] - 2))
                        pe.wait_ge(*released(PAIR0["out", i] - 1))
                    else:
                        pe.wait_ge(p_ev_lat, g)
                        if ctx:
                            pe.wait_ge(p_ev_ctx, CTXG(i) + h)
                    for kt in range(4):
                        for b in range(2):
                            last = nc.tensor.transpose(bank[kt // 2][:, (kt % 2) * SEQ + b * P:(kt % 2) * SEQ + (b + 1) * P],
                                                       PB[:, h % 2, b, kt * P:(kt + 1) * P], ident)
                    if ctx:
                        for kt in range(2):
                            for b in range(2):
                                last = nc.tensor.transpose(bank[2][:, kt * CTX + b * P:kt * CTX + (b + 1) * P],
                                                           PB[:, h % 2, 2, b * CTX + kt * P:b * CTX + (kt + 1) * P], ident)
                    last.then_inc(p_turned, 1)

                def pv(h):
                    g = G + h
                    if h > 0:
                        pe.wait_ge(ao_lo, g)
                    vc = (h // part) * P
                    pe.wait_ge(p_ev_lat, g + 1)
                    for kt in range(4):
                        last = mm(bank[3][:, 0:SEQ], VT[:, kt, vc:vc + P], PT[:, h % 2, kt // 2, (kt % 2) * SEQ:(kt % 2 + 1) * SEQ],
                                  start=(kt == 0), stop=(kt == 3))
                    if ctx:
                        pe.wait_ge(p_ev_ctx, CTXG(i) + h + 1)
                        for kt in range(2):
                            last = mm(bank[3][:, SEQ:TOK], VT[:, 2 + kt, vc:vc + P], PT[:, h % 2, 2, kt * CTX:(kt + 1) * CTX],
                                      start=(kt == 0), stop=(kt == 1))
                    last.then_inc(pv_done, 1)

                scores(0)
                if i == 0:
                    for x in AFTER_IN:
                        reduce_mod(x)
                for h in range(HEADS[i]):
                    if h + 1 < HEADS[i]:
                        scores(h + 1)
                    turn(h)
                    if h > 0:
                        pv(h - 1)
                        if i == 0:
                            for x in HEAD_MODS[h - 1]:
                                reduce_mod(x)
                pv(HEADS[i] - 1)
                if i == 0:
                    for x in HEAD_MODS[HEADS[i] - 1]:
                        reduce_mod(x)

            def filter_stage(t):
                if t < 3:
                    if t == 0:
                        pe.wait_ge(tab_in, TAB_AT[1])
                        pe.wait_ge(mod_final, 3)
                        mm(bank[6][0:FW, 0:SEQ], FWT[0:FEMB, 0:FW], FA[0:FEMB, 0, :], start=True, stop=True).then_inc(f_mm, 1)
                    else:
                        pe.wait_ge(f_sin, t)
                        w = FW if t == 1 else 2 * FW
                        mm(bank[6][0:w, 0:SEQ], FWT[0:FW, t * FW:t * FW + w], FA[0:FW, t % 2, :], start=True,
                           stop=True).then_inc(f_mm, 1)
                elif t < 7:
                    tt, hf = divmod(t - 3, 2)
                    pe.wait_ge(f_sin, 3)
                    if t > 3:
                        pe.wait_ge(f_h, t - 3)
                    for d in range(2):
                        ps = slice(FW * d, FW * d + FW)
                        last = mm(bank[6 + d], FA[ps, 1, tt * P:(tt + 1) * P], W4[ps, hf * 512:(hf + 1) * 512],
                                  start=True, stop=True)
                    last.then_inc(f_mm, 1)
                else:
                    pe.wait_ge(f_h, 4)
                    for x in range(2 * (t - 7), 2 * (t - 7) + 2):
                        j, hf = divmod(x, 2)
                        if x >= 2:
                            pe.wait_ge(f_sev, x - 1)
                        src = HD if j in (2, 3) else HS
                        blk = (0, 1, 5, 3, 4)[j]
                        for kt in range(2):
                            last = mm(bank[6 + x % 2], DF[:, kt, blk * P:(blk + 1) * P], src[:, kt, hf * 512:(hf + 1) * 512],
                                      start=(kt == 0), stop=(kt == 1))
                        last.then_inc(f_spec, 1)

            def long_conv():
                def turn(w):
                    hf, st = divmod(w, 2)
                    if w == 0:
                        pe.wait_ge(z_conv, 3 * KT)
                        pe.wait_ge(root_ready, ROOT["o", 2])
                    else:
                        pe.wait_ge(c_vt_act, w)
                        pe.wait_ge(c_vt_dve, w)
                    for tt in range(2):
                        for c in range(4):
                            last = nc.tensor.transpose(bank[4 + tt][:, c * P:(c + 1) * P],
                                                       XV[:, 4 * hf + c, st * SEQ + tt * P:st * SEQ + (tt + 1) * P], ident)
                    last.then_inc(c_turned, 1)

                def forward(w):
                    pe.wait_ge(c_vt_act, w + 1)
                    pe.wait_ge(c_vt_dve, w + 1)
                    if w == 0:
                        pe.wait_ge(*released(PAIR0["out", 1] - 1))
                    else:
                        pe.wait_ge(c_prod, 8 * w)
                    for j in range(4):
                        for tt in range(2):
                            last = mm(bank[j], DF[:, tt, j * P:(j + 1) * P], VX[:, w % 2, tt, :],
                                      start=(tt == 0), stop=(tt == 1))
                    last.then_inc(c_fwd, 1)

                def inverse(w):
                    pe.wait_ge(c_y, 4 * (w + 1))
                    if w == 0:
                        pe.wait_ge(tab_in, TAB_AT[1] + 16)
                        pe.wait_ge(f_sev, 10)
                    else:
                        pe.wait_ge(c_skip, 4 * w)
                    for c in range(4):
                        for j in range(4):
                            last = mm(bank[6 + c // 2][:, (c % 2) * SEQ:(c % 2 + 1) * SEQ], YS[:, w % 2, j, c * P:(c + 1) * P],
                                      IF[:, j, :], start=(j == 0), stop=(j == 3))
                    last.then_inc(c_inv, 1)

                turn(0)
                forward(0)
                turn(1)
                for w in range(4):
                    if w < 3:
                        forward(w + 1)
                    inverse(w)
                    if w < 2:
                        turn(w + 2)

            for i in range(DEPTH):
                N = NL[i]
                u_norm(2 * i)
                n0, q0 = FIRST["in", i], PAIR0["in", i]
                if KIND[i] == 1:
                    first_tiles(n0, q0, 2 * i, (TOK, TOK))
                    filter_stage(0)
                    filter_stage(1)
                    for t in range(2, 12):
                        tile(n0 + t, q0 + t, TOK, UH, UL, True, True)
                        filter_stage(t)
                    long_conv()
                    arrive = lambda k: pe.wait_ge(c_lo, 8 * (k // 4 + 1))
                else:
                    first_tiles(n0, q0, 2 * i, (N, N))
                    if N < TOK:
                        pe.wait_ge(*u_part(2 * i, 1, KT - 2))
                        pe.wait_ge(*u_part(2 * i, 1, KT - 1))
                    turn_q(i, 0)
                    turn_q(i, 1)
                    for t in range(2, 6):
                        tile(n0 + t, q0 + t, TOK if t >= 4 else N, UH, UL, True, True)
                        turn_q(i, 2 * t - 2)
                        turn_q(i, 2 * t - 1)
                    for j in range(VCH[i]):
                        turn_v(i, j)
                    attention(i)
                    G, per = ahead(HEADS, i), HEADS[i] // KT
                    arrive = lambda k, G=G, per=per: pe.wait_ge(ao_lo, G + per * (k + 1))
                n0, q0 = FIRST["out", i], PAIR0["out", i]
                for t in range(4):
                    tile(n0 + t, q0 + t, N, UH, UL, True, True, arrive=arrive if t == 0 else None)
                o_norm(2 * i)
                u_norm(2 * i + 1)
                n0, q0 = FIRST["up", i], PAIR0["up", i]
                first_tiles(n0, q0, 2 * i + 1, (N, N))
                for t in range(2, FM):
                    tile(n0 + t, q0 + t, N, UH, UL, True, True)
                n0, q0 = FIRST["down", i], PAIR0["down", i]
                for t in range(12):
                    pair, third = divmod(t, 3)
                    tile(n0 + t, q0 + pair, N, MH, ML, third == 0, third == 2, kt0=8 * third,
                         arrive=(lambda k, b=i * FM: pe.wait_ge(ml_ready, b + k + 1)) if pair == 0 else None)
                o_norm(2 * i + 1)

            for x in range(4):
                t, g = divmod(x, 2)
                for c in range(4):
                    if t == 0:
                        cc = 4 * g + c
                        pe.wait_ge(h_even if cc % 2 == 0 else h_odd, R0[-1] // 2 + cc // 2 + 1)
                    last = nc.tensor.transpose(bank[x][:, c * P:(c + 1) * P], H[:, 4 * g + c, t * P:(t + 1) * P], ident)
                last.then_inc(out_turned, 1)

        @block.scalar
        def _(act):
            f = nc.scalar.activation

            def hi(n):
                if n >= NT:
                    return
                words = TILES[n][3] * TILES[n][5]
                act.wait_ge(raw_in[n % 2], 16 * (n // 2 + 1))
                if n >= 2:
                    act.wait_ge(tile_done, n - 1)
                f(WH[:, n % 2, 0:words], RAW[:, n % 2, 0:words], ACT.Copy).then_inc(hi_ready, 1)

            def square(s, src, N, **kw):
                if s >= 2:
                    act.wait_ge(*USED[s - 2])
                f(SQ[:, s % 2, 0:N], src, ACT.Square, **kw).then_inc(sq_ready, 1)

            def root(s, src, dst):
                act.wait_ge(stat_step, s)
                f(dst, src, ACT.Sqrt, scale=1.0 / D, bias=eps[:, :]).then_inc(root_ready, 1)

            def o_root(k):
                N = NL[k // 2]
                root(SUMMED["o", k], bank[4][:, 0:N], RMS_O[:, 0:N])

            def pre_norm(k):
                for v in range(UV[k]):
                    s = slice(v * SEQ, (v + 1) * SEQ)
                    for c in range(KT):
                        if k == 0:
                            act.wait_ge(h_loaded, c + 1)
                        elif v < OV[k - 1]:
                            act.wait_ge(h_even if c % 2 == 0 else h_odd, R0[k - 1] // 2 + (KT // 2) * v + c // 2 + 1)
                        square(SQH[k] + KT * v + c, H[:, c, s], SEQ)
                    root(SUMMED["h", k, v], bank[6 + v][:, 0:SEQ], RMS_H[:, s])
                shift = 3 * KT * (k % 2)
                for v in range(UV[k]):
                    s = slice(v * SEQ, (v + 1) * SEQ)
                    for c in range(KT):
                        act.wait_ge(un_ready, U0[k] + KT * v + c + 1)
                        b = modv[:, v, shift + c:shift + c + 1]
                        if c % 2:
                            f(UH[:, c, s], TC[:, c, s], ACT.Identity, bias=b)
                            f(TC[:, c, s], TC[:, c, s], ACT.Identity, bias=b).then_inc(us_ready, 1)
                        else:
                            f(UH[:, c, s], TC[:, c, s], ACT.Identity, bias=b).then_inc(uh_ready, 1)

            def o_chunks(k, t, q, dst, N, bias, n):
                fn = ACT.Identity if bias else ACT.Copy

                def arg(m):
                    return {"bias": col(bias, 2 * t + m)} if bias else {}

                if t < 3:
                    hi(n)
                for m in range(2):
                    square(SQO[k] + 2 * t + m, bank[2 * (q % 2) + m][:, 0:N], N, **arg(m))
                if t == 3:
                    o_root(k)
                for m in range(2):
                    f(dst[:, 2 * t + m, 0:N], bank[2 * (q % 2) + m][:, 0:N], fn, **arg(m)).then_inc(o_ready, 1)
                if t == 3:
                    hi(n)

            act.wait_ge(par_ready, 2)
            act.wait_ge(consts_set, 1)
            f(S2[:, 0, :], col("c", 0, KT), ACT.Silu)
            f(S2[:, 1, :], col("c_ctx", 0, KT), ACT.Silu).then_inc(silu_ready, 1)
            for c in range(KT):
                act.wait_ge(x_turned, c + 1)
                f(H[:, c, :], bank[c % 4], ACT.Copy).then_inc(h_loaded, 1)
            hi(0)
            hi(1)
            for g in range(MOD0 // 4):
                act.wait_ge(group_done, g + 1)
                f(MROW[0:2, g * 512:(g + 1) * 512], bank[g % 4][0:2, :], ACT.Copy).then_inc(group_rows, 1)

            def attention_in(i):
                n0, q0, A = FIRST["in", i], PAIR0["in", i], KIND[i] == 0
                E = ahead(EV, i)

                def q_norm(r):
                    g = turns_ahead(i) + r
                    act.wait_ge(q_turned, g + 1)
                    if r == 7:
                        nb = NL[i] // P
                        f(q_scale[:, 0, :].rearrange("p (h b) -> p h b", b=4)[:, :, 0:nb],
                          bank[4][:, 0:4 * A_HEADS].rearrange("p (h b) -> p h b", b=4)[:, :, 0:nb], ACT.Sqrt,
                          scale=1.0 / A_DH, bias=eps[:, :]).then_inc(q_root, 1)
                    else:
                        f(CV[:, r % 2, :], bank[QSUM(i, r)], ACT.Sqrt, scale=1.0 / A_DH,
                          bias=eps[:, :]).then_inc(q_root, 1)

                for t in range(6):
                    act.wait_ge(tile_done, n0 + t + 1)
                    hi(n0 + t + 2)
                    b0 = 2 * ((q0 + t) % 2)
                    if A:
                        for m in range(2):
                            c = 2 * t + m
                            N = NL[i] if c < 8 else TOK
                            src = bank[b0 + m][:, 0:N]
                            if c < 10:
                                if c >= 2:
                                    act.wait_ge(q_turned, turns_ahead(i) + c - 1)
                                f(SQ[:, c % 2, 0:N], src, ACT.Square)
                                gain = col("a_q_gain" if c < 8 else "a_k_gain", i // 3)
                                f(QK[:, c, 0:N], src, ACT.Copy, scale=gain).then_inc(q_evac, 1)
                            else:
                                f(QK[:, c, :], src, ACT.Copy).then_inc(q_evac, 1)
                            if c == 9:
                                q_norm(7)
                    else:
                        for m in range(2 if t < 4 else 1):
                            c = 2 * t + m if t < 4 else t + 4
                            f(QK[:, c, :], bank[b0 + m], ACT.Identity, bias=col("c_b_qkv", c)).then_inc(q_evac, 1)
                for r in ((8, 9) if A else ()):
                    q_norm(r)
                for j in range(VCH[i]):
                    act.wait_ge(v_turned, ahead(VCH, i) + j + 1)
                    if A:
                        f(VT[:, :, j * P:(j + 1) * P], v_bank(i, j).rearrange("p (k d) -> p k d", k=4),
                          ACT.Copy).then_inc(v_ready, 1)
                    else:
                        src = v_bank(i, 0).rearrange("p (k g d) -> p k g d", k=4, g=2)
                        dst = VT[:, :, :].rearrange("p k (g u d) -> p k g u d", g=2, u=2)
                        f(dst[:, :, :, 0, :], src, ACT.Copy)
                        f(dst[:, :, :, 1, :], src, ACT.Copy).then_inc(v_ready, 1)

            def attention(i):
                G, A = ahead(HEADS, i), KIND[i] == 0
                ctx = NL[i] == TOK
                scale = (A_DH if A else C_DH) ** -0.5
                nE = 4 if ctx else 2

                def exps(h):
                    g, sl = G + h, small[:, h % 2, :, :]
                    act.wait_ge(s_max, g + 1)
                    if h >= 2:
                        act.wait_ge(p_turned, g - 1)
                    for b in range(nE):
                        nm, acc = sl[:, 1, b:b + 1], sl[:, 2, b:b + 1]
                        if b < 2:
                            dst = PB[:, h % 2, b, :]
                            src, sc = (bank[6 + b], q_scale[:, 0, 4 * h + b:4 * h + b + 1]) if A else (SM[:, b, :], 1.0)
                        else:
                            dst = PB[:, h % 2, 2, (b - 2) * CTX:(b - 1) * CTX]
                            src = bank[4][:, (b - 2) * CTX:(b - 1) * CTX]
                            sc = q_scale[:, 0, 4 * h + b:4 * h + b + 1] if A else scale
                        last = f(dst, src, ACT.Exp, scale=sc, bias=nm, accum_out=acc)
                    if not A:
                        last = f(sl[:, 4, 0:nE], sl[:, 1, 0:nE], ACT.Exp, bias=sinkb[:, h:h + 1])
                    last.then_inc(s_exp, 1)

                def evac(h):
                    g = G + h
                    act.wait_ge(p_turned, g + 1)
                    if h > 1:
                        act.wait_ge(pv_done, g - 1)
                    f(PT[:, h % 2, 0:2, :], lo4[:, 0:2, :], ACT.Copy).then_inc(p_ev_lat, 1)

                def o_hi(h):
                    g, N = G + h, NL[i]
                    act.wait_ge(pv_done, g + 1)
                    if A:
                        f(UH[:, h, 0:N], bank[3][:, 0:N], ACT.Copy).then_inc(ao_hi, 1)
                    else:
                        ps = slice(64 * (h % 2), 64 * (h % 2) + 64)
                        f(UH[ps, h // 2, 0:N], bank[3][ps, 0:N], ACT.Copy).then_inc(ao_hi, 1)

                exps(0)
                for h in range(HEADS[i]):
                    evac(h)
                    if h + 1 < HEADS[i]:
                        exps(h + 1)
                    if h > 0:
                        o_hi(h - 1)
                o_hi(HEADS[i] - 1)

            def hyena_in():
                n0, q0 = FIRST["in", 1], PAIR0["in", 1]
                for t in range(12):
                    act.wait_ge(tile_done, n0 + t + 1)
                    hi(n0 + t + 2)
                    for m in range(2):
                        c = 2 * t + m
                        if t < 4:
                            cm, dst = c, X0[:, c, :]
                        else:
                            s, isv = divmod(t - 4, 2)
                            cm = (8 + 8 * isv) + 2 * s + m
                            dst = VC[:, m, :] if isv else XV[:, 2 * s + m, :]
                        if c >= 2:
                            act.wait_ge(z_conv, c - 1)
                        f(CV[:, m, :], bank[2 * ((q0 + t) % 2) + m], ACT.Identity, bias=col("b_b_in", cm)).then_inc(z_evac, 1)
                        act.wait_ge(z_evac, c + 1)
                        f(dst, CV[:, m, :], ACT.Identity, scale=col("b_conv_w", 3 * KT + cm),
                          bias=col("b_conv_b", cm)).then_inc(z_tap, 1)
                    if t < 3:
                        act.wait_ge(f_arg, t + 1)
                        w = FW if t < 2 else 2 * FW
                        f(FA[0:w, (t + 1) % 2, :], FT[0:w, 0, :], ACT.Sin).then_inc(f_sin, 1)
                    elif t >= 7:
                        for x in range(2 * (t - 7), 2 * (t - 7) + 2):
                            j, hf = divmod(x, 2)
                            act.wait_ge(f_spec, x + 1)
                            f(BF[:, j, hf * 512:(hf + 1) * 512], bank[6 + x % 2], ACT.Copy).then_inc(f_sev, 1)

            def long_conv():
                def vt(w):
                    act.wait_ge(c_turned, w + 1)
                    if w >= 2:
                        act.wait_ge(c_fwd, w - 1)
                    f(VX[:, w % 2, 0, :], bank[4], ACT.Copy).then_inc(c_vt_act, 1)

                def part(w):
                    hf, st = divmod(w, 2)
                    for c in range(4):
                        act.wait_ge(c_gated, 4 * w + c + 1)
                        f(UH[:, 4 * hf + c, st * SEQ:(st + 1) * SEQ], XV[:, 4 * hf + c, st * SEQ:(st + 1) * SEQ],
                          ACT.Copy).then_inc(c_hi, 1)

                vt(0)
                vt(1)
                for w in range(4):
                    if w < 2:
                        part(w)
                        vt(w + 2)
                    else:
                        part(w)

            for i in range(DEPTH):
                N = NL[i]
                pre_norm(2 * i)
                if KIND[i] == 1:
                    hyena_in()
                    long_conv()
                else:
                    attention_in(i)
                    attention(i)
                n0, q0 = FIRST["out", i], PAIR0["out", i]
                for t in range(4):
                    act.wait_ge(tile_done, n0 + t + 1)
                    o_chunks(2 * i, t, q0 + t, OM, N, (None, "b_b_out", "c_b_out")[KIND[i]], n0 + t + 2)
                pre_norm(2 * i + 1)
                n0, q0 = FIRST["up", i], PAIR0["up", i]
                for s in range(FM // 2):
                    g = n0 + 2 * s
                    act.wait_ge(tile_done, g + 1)
                    hi(g + 2)
                    for m in range(2):
                        c = 2 * s + m
                        if c >= 2:
                            act.wait_ge(ml_ready, i * FM + c - 1)
                        f(CV[:, m, 0:N], bank[2 * ((q0 + 2 * s) % 2) + m][:, 0:N], ACT.Identity,
                          scale=col("ffn_conv_w", (3 * i + 1) * FM + c), bias=col("ffn_conv_b", i * FM + c)).then_inc(tap0, 1)
                    for m in range(2):
                        c = 2 * s + m
                        act.wait_ge(conv_done, i * FM + c + 1)
                        f(CV[:, m, 0:N], CV[:, m, 0:N], ACT.Silu).then_inc(silu_done, 1)
                    act.wait_ge(tile_done, g + 2)
                    hi(g + 3)
                    for m in range(2):
                        c = 2 * s + m
                        act.wait_ge(mf_ready, i * FM + c + 1)
                        f(MH[:, c, 0:N], CV[:, m, 0:N], ACT.Copy).then_inc(mh_ready, 1)
                n0, q0 = FIRST["down", i], PAIR0["down", i]
                for t in range(12):
                    pair, third = divmod(t, 3)
                    act.wait_ge(tile_done, n0 + t + 1)
                    if third == 2:
                        o_chunks(2 * i + 1, pair, q0 + pair, OF, N, None, n0 + t + 2)
                    else:
                        hi(n0 + t + 2)

            for x in (1, 3):
                act.wait_ge(out_turned, x + 1)
                act.wait_ge(out_copied, x)
                f(XR[:, x // 2, 512:1024], bank[x], ACT.Copy).then_inc(out_copied, 1)

        @block.vector
        def _(dve):
            tt, ts, stt = nc.vector.tensor_tensor, nc.vector.tensor_scalar, nc.vector.scalar_tensor_tensor
            chained = [0]

            def link(ins):
                chained[0] += 1
                ins.then_inc(dve_chain, 1)
                dve.wait_ge(dve_chain, chained[0])

            def lo(n):
                if n >= NT:
                    return
                words = TILES[n][3] * TILES[n][5]
                dve.wait_ge(hi_ready, n + 1)
                tt(WL[:, n % 2, 0:words], RAW[:, n % 2, 0:words], WH[:, n % 2, 0:words].bitcast(F32),
                   ALU.subtract).then_inc(lo_ready, 1)

            def mod(k):
                dve.wait_ge(mod_in[k % 2], 16 * ((k - MOD0) // 2 + 1))
                if k % 2 == 0 and k >= MOD0 + 4:
                    dve.wait_ge(mod_reduced, (k - MOD0) // 2 - 1)
                for j in range(4):
                    for v in range(2):
                        s = S2[:, v, 4 * (k % 2) + j:4 * (k % 2) + j + 1]
                        acc = MA[:, k // 2 % 2, v, :]
                        if j == 0 and k % 2 == 0:
                            ts(acc, MR[:, k % 2, j, :], s, None, ALU.mult).then_inc(mod_step, 1)
                        else:
                            dve.wait_ge(mod_step, 8 * (k - MOD0) + 2 * j + v - 1)
                            stt(acc, MR[:, k % 2, j, :], s, acc, ALU.mult, ALU.add).then_inc(mod_step, 1)

            def finish_mod(i, part):
                W = NMOD * KT
                c0, c1 = (0, W) if i else ((0, 3 * KT), (3 * KT, W))[part]
                if i or part:
                    dve.wait_ge(mod_reduced, MB * (i + 1) - MOD0 // 2)
                else:
                    dve.wait_ge(group_cols, 1)
                for v in range(2):
                    ins = tt(modv[:, v, c0:c1], modp[:, v * W + c0:v * W + c1], col("mod_b", i * W + c0, c1 - c0), ALU.add)
                link(ins)
                for v in range(2):
                    g = [col("norm_g", (4 * i + n) * KT, KT) for n in range(4)]
                    m = [modv[:, v, j * KT:(j + 1) * KT] for j in range(NMOD)]
                    if c0 == 0:
                        stt(coef[:, v, 0, :], m[1], 1.0, g[0], ALU.add, ALU.mult)
                        ins = tt(coef[:, v, 1, :], m[2], g[1], ALU.mult)
                    if c1 == W:
                        stt(coef[:, v, 2, :], m[4], 1.0, g[2], ALU.add, ALU.mult)
                        ins = tt(coef[:, v, 3, :], m[5], g[3], ALU.mult)
                ins.then_inc(mod_final, 1)
                dve.wait_ge(mod_final, i + 2 if i else part + 1)

            def residual(k, O):
                dve.wait_ge(root_ready, ROOT["o", k] + 1)
                for v in range(OV[k]):
                    s = slice(v * SEQ, (v + 1) * SEQ)
                    link(nc.vector.reciprocal(RMS_O[:, s], RMS_O[:, s]))

                    def scaled(c):
                        stt(TC[:, c, s], O[:, c, s], coef[:, v, 1 + 2 * (k % 2), c:c + 1], RMS_O[:, s], ALU.mult,
                            ALU.mult).then_inc(gated, 1)

                    def add(c):
                        dve.wait_ge(gated, R0[k] + KT * v + c + 1)
                        tt(H[:, c, s], H[:, c, s], TC[:, c, s], ALU.add).then_inc(h_even, 1)

                    for c in range(KT):
                        dve.wait_ge(o_ready, k * KT + c + 1)
                        scaled(c)
                        if c % 2 == 1:
                            add(c - 1)

            def pre_norm(k):
                shift = 3 * KT * (k % 2)
                if k > 0:
                    dve.wait_ge(h_odd, (R0[k - 1] + KT * OV[k - 1]) // 2)
                for v in range(UV[k]):
                    s = slice(v * SEQ, (v + 1) * SEQ)

                    def scaled(c):
                        stt(TC[:, c, s], H[:, c, s], coef[:, v, 2 * (k % 2), c:c + 1], RMS_H[:, s], ALU.mult,
                            ALU.mult).then_inc(un_ready, 1)

                    def low(c):
                        dve.wait_ge(uh_ready, (U0[k] + KT * v) // 2 + c // 2 + 1)
                        stt(UL[:, c, s], TC[:, c, s], modv[:, v, shift + c:shift + c + 1], UH[:, c, s].bitcast(F32),
                            ALU.add, ALU.subtract).then_inc(u_even, 1)

                    dve.wait_ge(root_ready, ROOT["h", k, v] + 1)
                    link(nc.vector.reciprocal(RMS_H[:, s], RMS_H[:, s]))
                    scaled(0)
                    scaled(1)
                    for c in range(0, KT, 2):
                        if c + 2 < KT:
                            scaled(c + 2)
                            scaled(c + 3)
                        low(c)

            nc.vector.memset(eps[:, :], EPS)
            nc.vector.memset(ones[:, :], 1.0).then_inc(consts_set, 1)
            dve.wait_ge(par_turned, 1)
            nc.vector.tensor_copy(par[:, 0:512], bank[6])
            nc.vector.tensor_copy(par[:, 512:NPAR * P], bank[7][:, 0:NPAR * P - 512]).then_inc(par_ready, 2)
            dve.wait_ge(silu_ready, 1)
            dve.wait_ge(par_ready, 2)
            lo(0)
            lo(1)
            finish_mod(0, 0)
            dve.wait_ge(h_loaded, KT)

            def rope(i, t):
                for r in (2 * t, 2 * t + 1):
                    g = turns_ahead(i) + r
                    N = NL[i] if r < 8 else TOK
                    turned = turned_bank(i, r)[:, 0:N]
                    tmp = RT[:, r % 2, 0:N]
                    if KIND[i] == 0 and r >= 8:
                        dve.wait_ge(q_root, norms_ahead(i) + r - 6)
                        nc.vector.reciprocal(CV[:, r % 2, 0:N], CV[:, r % 2, 0:N])
                    dve.wait_ge(q_turned, g + 1)
                    link(tt(tmp, turned, sinT[:, 0:N], ALU.mult))
                    if KIND[i] == 0 and r >= 8:
                        dve.wait_ge(q_cos, QCOS(i) + r + 1)
                        link(tt(tmp, tmp, QK[:, r, 0:N], ALU.add))
                        tt(QK[:, r, 0:N], tmp, CV[:, r % 2, 0:N], ALU.mult).then_inc(q_roped, 1)
                    elif r < 8:
                        dve.wait_ge(q_cos, QCOS(i) + r + 1)
                        tt(QK[:, r, 0:N], tmp, QK[:, r, 0:N], ALU.add).then_inc(q_roped, 1)
                    else:
                        link(tt(KD[:, r - 8, :], bank[4 + r % 2], cosT, ALU.mult))
                        tt(KD[:, r - 8, :], KD[:, r - 8, :], tmp, ALU.add).then_inc(q_roped, 1)

            def attention_in(i):
                n0 = FIRST["in", i]
                for t in range(6):
                    lo(n0 + t + 2)
                    if t == 0:
                        dve.wait_ge(*((tab_in, TAB_AT[i]) if i else (start_in, 32)))
                    if t > 0:
                        rope(i, t - 1)
                    for x in mods_at(n0 + t):
                        mod(x)

            def attention(i):
                G, A = ahead(HEADS, i), KIND[i] == 0
                ctx = NL[i] == TOK
                scale = (A_DH if A else C_DH) ** -0.5
                nE = 4 if ctx else 2

                def maxima(h):
                    g, sl = G + h, small[:, h % 2, :, :]
                    dve.wait_ge(s_ready, g + 1)
                    if h >= 2 or (h and not A):
                        dve.wait_ge(s_exp, g - 1 if A else g)
                    if A:
                        ins = nc.vector.tensor_reduce(sl[:, 0, 0:2], hi2[:, :, :], AX.X, ALU.max)
                    else:
                        for b in range(2):
                            ins = nc.vector.tensor_tensor_reduce(SM[:, b, :], hi2[:, b, :], maskT[:, b, :], scale, -3e38,
                                                                 ALU.add, ALU.max, sl[:, 0, b:b + 1])
                        ins.then_inc(s_masked, 1)
                    if ctx:
                        ins = nc.vector.tensor_reduce(sl[:, 0, 2:4], bank[4].rearrange("p (b k) -> p b k", b=2), AX.X, ALU.max)
                    if A:
                        link(ins)
                        tt(sl[:, 1, 0:nE], sl[:, 0, 0:nE], q_scale[:, 1, 4 * h:4 * h + nE], ALU.mult).then_inc(s_max, 1)
                    else:
                        if ctx:
                            link(ins)
                            link(ts(sl[:, 0, 2:4], sl[:, 0, 2:4], scale, None, ALU.mult))
                        dve.wait_ge(s_masked, MASKED(i) + h + 1)
                        ts(sl[:, 1, 0:nE], sl[:, 0, 0:nE], sinkb[:, h:h + 1], -1.0, ALU.max, ALU.mult).then_inc(s_max, 1)

                def normalise(h):
                    g, sl = G + h, small[:, h % 2, :, :]
                    dve.wait_ge(s_exp, g + 1)
                    if not A:
                        link(tt(sl[:, 2, 0:nE], sl[:, 2, 0:nE], sl[:, 4, 0:nE], ALU.add))
                    link(nc.vector.reciprocal(sl[:, 3, 0:nE], sl[:, 2, 0:nE]))
                    for b in range(nE):
                        p = PB[:, h % 2, b, :] if b < 2 else PB[:, h % 2, 2, (b - 2) * CTX:(b - 1) * CTX]
                        ins = ts(p, p, sl[:, 3, b:b + 1], None, ALU.mult)
                    ins.then_inc(s_norm, 1)

                def evac(h):
                    g = G + h
                    if ctx:
                        dve.wait_ge(p_turned, g + 1)
                        if h > 1:
                            dve.wait_ge(pv_done, g - 1)
                        nc.vector.tensor_copy(PT[:, h % 2, 2, :], bank[2]).then_inc(p_ev_ctx, 1)

                def o_lo(h):
                    g, N = G + h, NL[i]
                    dve.wait_ge(ao_hi, g + 1)
                    ps, c = (slice(0, P), h) if A else (slice(64 * (h % 2), 64 * (h % 2) + 64), h // 2)
                    tt(UL[ps, c, 0:N], bank[3][ps, 0:N], UH[ps, c, 0:N].bitcast(F32), ALU.subtract).then_inc(ao_lo, 1)

                if A:
                    dve.wait_ge(q_root, norms_ahead(i) + 1)
                    q3 = [q_scale[:, x, :].rearrange("p (h b) -> p h b", b=4)[:, :, 0:nE] for x in range(2)]
                    link(nc.vector.reciprocal(q3[0], q3[0]))
                    link(ts(q3[1], q3[0], -scale, None, ALU.mult))
                    link(ts(q3[0], q3[0], scale, None, ALU.mult))
                maxima(0)
                normalise(0)
                for h in range(HEADS[i]):
                    if h + 1 < HEADS[i]:
                        maxima(h + 1)
                    evac(h)
                    if h + 1 < HEADS[i]:
                        normalise(h + 1)
                    if h > 0:
                        o_lo(h - 1)
                    if i == 0:
                        for x in HEAD_MODS[h]:
                            mod(x)
                o_lo(HEADS[i] - 1)

            def hyena_in():
                n0 = FIRST["in", 1]
                TWO_PI = 2.0 * math.pi
                C1 = 6.28125
                MAGIC = 1.5 * 2.0 ** 23
                for t in range(12):
                    lo(n0 + t + 2)
                    for m in range(2):
                        c = 2 * t + m
                        if t < 4:
                            cm, dst = c, X0[:, c, :]
                        else:
                            s, isv = divmod(t - 4, 2)
                            cm = (8 + 8 * isv) + 2 * s + m
                            dst = VC[:, m, :] if isv else XV[:, 2 * s + m, :]
                        d3, z3 = dst.rearrange("p (v t) -> p v t", v=2), CV[:, m, :].rearrange("p (v t) -> p v t", v=2)
                        dve.wait_ge(z_tap, c + 1)
                        link(stt(d3[:, :, 1:SEQ], z3[:, :, 0:SEQ - 1], col("b_conv_w", cm), d3[:, :, 1:SEQ], ALU.mult, ALU.add))
                        ins = stt(d3[:, :, 0:SEQ - 1], z3[:, :, 1:SEQ], col("b_conv_w", 6 * KT + cm), d3[:, :, 0:SEQ - 1],
                                  ALU.mult, ALU.add)
                        if t >= 4 and isv:
                            link(ins)
                            xv = XV[:, 2 * s + m, :]
                            tt(xv, xv, dst, ALU.mult).then_inc(z_conv, 1)
                        else:
                            ins.then_inc(z_conv, 1)
                    if t < 3:
                        w = FW if t < 2 else 2 * FW
                        x, n = FT[0:w, 0, :], FT[0:w, 1, :]
                        dve.wait_ge(f_mm, t + 1)
                        if t > 0:
                            dve.wait_ge(f_sin, t)
                        link(ts(x, bank[6][0:w, 0:SEQ], FBI[0:w, t:t + 1], None, ALU.add))
                        link(ts(n, x, 1.0 / TWO_PI, MAGIC, ALU.mult, ALU.add))
                        link(ts(n, n, -MAGIC, None, ALU.add))
                        link(stt(x, n, -C1, x, ALU.mult, ALU.add))
                        link(stt(x, n, -(TWO_PI - C1), x, ALU.mult, ALU.add))
                        ts(x, x, 3.1415925, -3.1415925, ALU.min, ALU.max).then_inc(f_arg, 1)
                    elif t < 7:
                        blk, hf = divmod(t - 3, 2)
                        s = slice(hf * 512, (hf + 1) * 512)
                        dve.wait_ge(f_mm, t + 1)
                        tt(HS[:, blk, s], bank[6], DC[:, blk, s], ALU.mult)
                        if blk == 0:
                            link(stt(HD[:, blk, s], bank[7], not_first, DC[:, blk, s], ALU.mult, ALU.mult))
                        else:
                            link(tt(HD[:, blk, s], bank[7], DC[:, blk, s], ALU.mult))
                        link(tt(HS[:, blk, s], HS[:, blk, s], HD[:, blk, s], ALU.add))
                        stt(HD[:, blk, s], HD[:, blk, s], -2.0, HS[:, blk, s], ALU.mult, ALU.add).then_inc(f_h, 1)

            def long_conv():
                def vt(w):
                    dve.wait_ge(c_turned, w + 1)
                    if w >= 2:
                        dve.wait_ge(c_fwd, w - 1)
                    nc.vector.tensor_copy(VX[:, w % 2, 1, :], bank[5]).then_inc(c_vt_dve, 1)

                def products(w):
                    hf, st = divmod(w, 2)
                    s = slice(hf * 512, (hf + 1) * 512)
                    dve.wait_ge(c_fwd, w + 1)
                    if w == 0:
                        dve.wait_ge(f_sev, 10)
                    if w >= 2:
                        dve.wait_ge(c_inv, w - 1)
                    tmp = [SQ[:, 0, :], SQ[:, 1, :], CV[:, 0, :], CV[:, 1, :]]
                    for b in range(2):
                        re, im, re2 = BF[:, b, s], BF[:, 2 + b, s], BF[:, 4 if b == 0 else 1, s]
                        ar, ai = bank[b], bank[2 + b]
                        tt(YS[:, w % 2, b, :], ar, re, ALU.mult).then_inc(c_prod, 1)
                        if w > 0:
                            dve.wait_ge(c_y, 4 * (w - 1) + 2 * b + 1)
                        tt(tmp[2 * b], ai, im, ALU.mult).then_inc(c_prod, 1)
                        tt(YS[:, w % 2, 2 + b, :], ar, im, ALU.mult).then_inc(c_prod, 1)
                        if w > 0:
                            dve.wait_ge(c_y, 4 * (w - 1) + 2 * b + 2)
                        tt(tmp[2 * b + 1], ai, re2, ALU.mult).then_inc(c_prod, 1)

                def skip(w):
                    hf, st = divmod(w, 2)
                    dve.wait_ge(c_inv, w + 1)
                    for c in range(4):
                        x = XV[:, 4 * hf + c, st * SEQ:(st + 1) * SEQ]
                        stt(x, x, col("b_skip", 4 * hf + c), bank[6 + c // 2][:, (c % 2) * SEQ:(c % 2 + 1) * SEQ],
                            ALU.mult, ALU.add).then_inc(c_skip, 1)

                vt(0)
                products(0)
                vt(1)
                for w in range(4):
                    if w < 3:
                        products(w + 1)
                    skip(w)
                    if w < 2:
                        vt(w + 2)

            for i in range(DEPTH):
                N = NL[i]
                pre_norm(2 * i)
                if KIND[i] == 1:
                    hyena_in()
                    long_conv()
                else:
                    attention_in(i)
                    attention(i)
                n0 = FIRST["out", i]
                for t in range(4):
                    if t < 3:
                        lo(n0 + t + 2)
                    for k in mods_at(n0 + t):
                        mod(k)
                residual(2 * i, OM)
                if i == 0:
                    finish_mod(0, 1)
                pre_norm(2 * i + 1)
                n0, q0 = FIRST["up", i], PAIR0["up", i]
                V = N // SEQ

                def halves(x):
                    return x[:, 0:N].rearrange("p (v t) -> p v t", v=V)

                for s in range(FM // 2):
                    lo(n0 + 2 * s + 2)
                    gate = [halves(bank[2 * ((q0 + 2 * s) % 2) + m]) for m in range(2)]
                    conv = [halves(CV[:, m, :]) for m in range(2)]
                    for m in range(2):
                        c = 2 * s + m
                        dve.wait_ge(tap0, i * FM + c + 1)
                        stt(conv[m][:, :, 1:SEQ], gate[m][:, :, 0:SEQ - 1], col("ffn_conv_w", 3 * i * FM + c),
                            conv[m][:, :, 1:SEQ], ALU.mult, ALU.add).then_inc(tap1, 1)
                    for m in range(2):
                        c = 2 * s + m
                        dve.wait_ge(tap1, i * FM + c + 1)
                        stt(conv[m][:, :, 0:SEQ - 1], gate[m][:, :, 1:SEQ], col("ffn_conv_w", (3 * i + 2) * FM + c),
                            conv[m][:, :, 0:SEQ - 1], ALU.mult, ALU.add).then_inc(conv_done, 1)
                    for k in mods_at(n0 + 2 * s):
                        mod(k)
                    lo(n0 + 2 * s + 3)
                    for m in range(2):
                        c = 2 * s + m
                        dve.wait_ge(tile_done, n0 + 2 * s + 2)
                        dve.wait_ge(silu_done, i * FM + c + 1)
                        tt(CV[:, m, 0:N], CV[:, m, 0:N], bank[2 * ((q0 + 2 * s + 1) % 2) + m][:, 0:N],
                           ALU.mult).then_inc(mf_ready, 1)
                    for k in mods_at(n0 + 2 * s + 1):
                        mod(k)
                n0 = FIRST["down", i]
                for t in range(12):
                    if t < 11:
                        lo(n0 + t + 2)
                    for k in mods_at(n0 + t):
                        mod(k)
                residual(2 * i + 1, OF)
                if i + 1 < DEPTH:
                    finish_mod(i + 1, 0)
            for x in (0, 2):
                dve.wait_ge(out_turned, x + 1)
                if x:
                    dve.wait_ge(out_copied, x)
                nc.vector.tensor_copy(XR[:, x // 2, 0:512], bank[x]).then_inc(out_copied, 1)

        @block.gpsimd
        def _(pool):
            tt = nc.gpsimd.tensor_tensor
            nc.gpsimd.memset(PR[:, :, :], 0.0).then_inc(rows_clear, 1)

            def o_squares(k):
                N = NL[k // 2]
                pool.wait_ge(sq_ready, SQO[k] + 2)
                if k > 0:
                    pool.wait_ge(stat_step, SUMMED["o", k - 1] - 2)
                tt(SQA[:, 0:N], SQ[:, 0, 0:N], SQ[:, 1, 0:N], ALU.add).then_inc(sq_added, 1)
                for c in range(2, KT - 2):
                    pool.wait_ge(sq_ready, SQO[k] + c + 1)
                    pool.wait_ge(sq_added, k * (KT - 3) + c - 1)
                    tt(SQA[:, 0:N], SQA[:, 0:N], SQ[:, c % 2, 0:N], ALU.add).then_inc(sq_added, 1)

            def residual(k):
                for v in range(OV[k]):
                    s = slice(v * SEQ, (v + 1) * SEQ)
                    for c in range(1, KT, 2):
                        pool.wait_ge(gated, R0[k] + KT * v + c + 1)
                        tt(H[:, c, s], H[:, c, s], TC[:, c, s], ALU.add).then_inc(h_odd, 1)
                n = FIRST["up", k // 2] + 1 if k % 2 == 0 else FIRST["down", k // 2] + 13
                if n < NT:
                    words = TILES[n][3] * TILES[n][5]
                    pool.wait_ge(hi_ready, n + 1)
                    tt(WL[:, n % 2, 0:words], RAW[:, n % 2, 0:words], WH[:, n % 2, 0:words].bitcast(F32),
                       ALU.subtract).then_inc(lo_ready, 1)

            def pre_norm(k):
                for v in range(UV[k]):
                    s = slice(v * SEQ, (v + 1) * SEQ)
                    for c in range(1, KT, 2):
                        pool.wait_ge(us_ready, (U0[k] + KT * v) // 2 + c // 2 + 1)
                        tt(UL[:, c, s], TC[:, c, s], UH[:, c, s].bitcast(F32), ALU.subtract).then_inc(u_odd, 1)

            def attention_in(i):
                pool.wait_ge(*((tab_in, TAB_AT[i]) if i else (start_in, 32)))
                for r in range(10 if KIND[i] == 0 else 8):
                    N = NL[i] if r < 8 else TOK
                    pool.wait_ge(q_turned, turns_ahead(i) + r + 1)
                    tt(QK[:, r, 0:N], QK[:, r, 0:N], cosT[:, 0:N], ALU.mult).then_inc(q_cos, 1)

            def long_conv():
                pool.wait_ge(f_h, 4)
                pool.dma_start(IF[:, :, :], a["k_idft"].rearrange("(j p) t -> p j t", p=P)).then_inc(tab_in, 16)

                def y(w):
                    tmp = [SQ[:, 0, :], SQ[:, 1, :], CV[:, 0, :], CV[:, 1, :]]
                    for b in range(2):
                        pool.wait_ge(c_prod, 8 * w + 4 * b + 2)
                        y = YS[:, w % 2, b, :]
                        tt(y, y, tmp[2 * b], ALU.subtract).then_inc(c_y, 1)
                        pool.wait_ge(c_prod, 8 * w + 4 * b + 4)
                        y = YS[:, w % 2, 2 + b, :]
                        tt(y, y, tmp[2 * b + 1], ALU.add).then_inc(c_y, 1)

                def gate(w):
                    hf, st = divmod(w, 2)
                    s = slice(st * SEQ, (st + 1) * SEQ)
                    for c in range(4):
                        pool.wait_ge(c_skip, 4 * w + c + 1)
                        tt(XV[:, 4 * hf + c, s], XV[:, 4 * hf + c, s], X0[:, 4 * hf + c, s], ALU.mult).then_inc(c_gated, 1)
                    for c in range(4):
                        pool.wait_ge(c_hi, 4 * w + c + 1)
                        tt(UL[:, 4 * hf + c, s], XV[:, 4 * hf + c, s], UH[:, 4 * hf + c, s].bitcast(F32),
                           ALU.subtract).then_inc(c_lo, 1)

                y(0)
                for w in range(4):
                    if w < 3:
                        y(w + 1)
                    gate(w)

            def load_tables(i):
                pool.wait_ge(tile_done, FIRST["in", i])
                if KIND[i] == 0:
                    pool.dma_start(RC[:, 0:2 * TOK + P], a["k_rope_a"]).then_inc(tab_in, 16)
                elif KIND[i] == 2:
                    pool.dma_start(RC[:, :], a["k_rope_c"]).then_inc(tab_in, 16)

            def load_filter():
                pool.wait_ge(*u_part(2, 1, KT - 2))
                for dst, src in ((FA[0:FEMB, 0, :], a["k_zt"]), (FWT[0:FEMB, 0:FW], a["b_f_w1"][0]),
                                 (FWT[0:FW, FW:2 * FW], a["b_f_w2"][0]), (FWT[0:FW, 2 * FW:3 * FW], a["b_f_w3"][0]),
                                 (FWT[0:FW, 3 * FW:4 * FW], a["b_f_w3"][0]),
                                 (FBI[0:FW, 0:1], a["b_f_b1"].rearrange("o f -> f o")),
                                 (FBI[0:FW, 1:2], a["b_f_b2"].rearrange("o f -> f o")),
                                 (FBI[0:FW, 2:3], a["b_f_b3"].rearrange("o f -> f o")),
                                 (FBI[FW:2 * FW, 2:3], a["b_f_b3"].rearrange("o f -> f o")),
                                 (W4[0:FW, :], a["b_f_w4"][0, :, 0:D]), (W4[FW:2 * FW, :], a["b_f_w4"][0, :, D:2 * D]),
                                 (DC[:, :, :], a["k_decay"].rearrange("(b p) d -> p b d", p=P)),
                                 (DF[:, :, :], a["k_dft"].rearrange("(b p) d -> p b d", p=P))):
                    pool.dma_start(dst, src).then_inc(tab_in, 16)

            for i in range(DEPTH):
                N = NL[i]
                pre_norm(2 * i)
                if i > 0:
                    load_tables(i)
                if KIND[i] == 1:
                    load_filter()
                    long_conv()
                else:
                    attention_in(i)
                o_squares(2 * i)
                residual(2 * i)
                pre_norm(2 * i + 1)
                for c in range(FM):
                    pool.wait_ge(mh_ready, i * FM + c + 1)
                    tt(ML[:, c, 0:N], CV[:, c % 2, 0:N], MH[:, c, 0:N].bitcast(F32), ALU.subtract).then_inc(ml_ready, 1)
                o_squares(2 * i + 1)
                residual(2 * i + 1)


SLAB_AT = 8320
MOD0 = 24
ROPE_COLS = 2 * TOK + 5 * P + 2 * TOK
N_ROW_DMAS = sum((ROW0[name] + k - 1) // P - ROW0[name] // P + 1 for name, k in ROWS)
TAB_AT = {1: 16 * 13, 2: 16 * 15, 3: 16 * 16}


def QSUM(i, r):
    return 4 + (r % 2 if i else 0)


def QCOS(i):
    return sum(10 if KIND[j] == 0 else 8 for j in range(i) if KIND[j] != 1)


def MASKED(i):
    return sum(C_HEADS for j in range(i) if KIND[j] == 2)


def CTXG(i):
    return sum({0: A_HEADS, 1: 0, 2: C_HEADS}[KIND[j]] for j in range(i))


_INS = ["x", "c", "ctx", "c_ctx", "mod_w", "mod_b", "norm_g", "ffn_w_up", "ffn_conv_w", "ffn_conv_b", "ffn_w_down",
        "a_w_qkv", "a_q_gain", "a_k_gain", "a_w_out", "b_w_in", "b_b_in", "b_conv_w", "b_conv_b", "b_f_w1", "b_f_b1",
        "b_f_w2", "b_f_b2", "b_f_w3", "b_f_b3", "b_f_w4", "b_skip", "b_w_out", "b_b_out", "c_w_qkv", "c_b_qkv",
        "c_sink", "c_w_out", "c_b_out"]


def kernel(**inputs):
    import concourse.bacc as bacc
    from concourse.bass_utils import run_bass_kernel_spmd

    nc = bacc.Bacc("TRN2", target_bir_lowering=False, num_devices=1,
                   dynamic_dma_scratch_size=8192)
    arrays = {name: np.ascontiguousarray(inputs[name]) for name in _INS}
    arrays.update(constants())
    aps = {name: nc.dram_tensor("in_" + name, v.shape, mybir.dt.from_np(v.dtype), kind="ExternalInput").ap()
           for name, v in arrays.items()}
    out = nc.dram_tensor("out_0", (1, SEQ, D), F32, kind="ExternalOutput").ap()
    build(nc, aps, out)
    r = run_bass_kernel_spmd(nc, [{"in_" + name: v for name, v in arrays.items()}], core_ids=[0])
    return r.results[0]["out_0"]
```
